# Optimizing a Trainium2 kernel written in Bass

```python
import math
import jax
import jax.numpy as jnp
from jax import lax
import numpy as np

D_MODEL = 1024
BATCH = 1
SEQ = 256
DEPTH = 2

PLE_DIM = 256
NORM_EPS = 1e-6
N_EVEN = (DEPTH + 1) // 2
N_ODD = DEPTH // 2
CHUNK = 64
MIX_WIDTH = D_MODEL
GLA_HEADS = 4
GLA_DV = MIX_WIDTH // (2 * GLA_HEADS)
GLA_DK = GLA_DV // 2
GLA_GATE_RANK = 16
GLA_GATE_NORM = 16.0
RET_HEADS = 4
RET_DV = MIX_WIDTH // (2 * RET_HEADS)
RET_DK = RET_DV // 2
ROPE_BASE = 10000.0
EVEN_SPLIT_SIZES = (GLA_HEADS * GLA_DK, GLA_HEADS * GLA_DK, GLA_HEADS * GLA_DV, GLA_HEADS * GLA_DV, GLA_GATE_RANK, RET_HEADS * RET_DK, RET_HEADS * RET_DK, RET_HEADS * RET_DV, RET_HEADS * RET_DV)
EVEN_PROJ = sum(EVEN_SPLIT_SIZES)
POOL_WINDOWS = (2, 4, 8, 16)
POOL_GROUPS = 4
POOL_WIDTH = MIX_WIDTH // 2
POOL_GROUP_WIDTH = POOL_WIDTH // POOL_GROUPS
S5_H = 16
S5_P = 64
S5_WIDTH = MIX_WIDTH - POOL_WIDTH
S5_GROUPS = S5_WIDTH // S5_H
DT_MIN = 1e-3
DT_MAX = 1e-1
PEER_HEADS = 8
PEER_NKEYS = 128
PEER_EXPERTS = PEER_NKEYS * PEER_NKEYS
PEER_TOPK = 16
PEER_DKEY = 256
PEER_BLOCK = 128

kernel_name = 'hybrid_gla_retnet_pool_s5_peer'

def rms_norm(x, w):
    xf = x.astype(jnp.float32)
    y = xf * lax.rsqrt(jnp.mean(xf * xf, axis=-1, keepdims=True) + NORM_EPS)
    return (y * w.astype(jnp.float32)).astype(x.dtype)

def group_norm(x):
    xf = x.astype(jnp.float32)
    mu = jnp.mean(xf, axis=-1, keepdims=True)
    var = jnp.mean(jnp.square(xf - mu), axis=-1, keepdims=True)
    return (xf - mu) * lax.rsqrt(var + NORM_EPS)

def to_heads(t, n_heads):
    b, s, _ = t.shape
    return t.reshape(b, s, n_heads, -1).transpose(0, 2, 1, 3)

def from_heads(t):
    b, h, s, d = t.shape
    return t.transpose(0, 2, 1, 3).reshape(b, s, h * d)

def rotary(x, positions):
    half = x.shape[-1] // 2
    freqs = ROPE_BASE ** (-jnp.arange(half, dtype=jnp.float32) / half)
    ang = positions.astype(jnp.float32)[:, None] * freqs[None, :]
    cos, sin = jnp.cos(ang), jnp.sin(ang)
    xf = x.astype(jnp.float32)
    x1, x2 = xf[..., :half], xf[..., half:]
    return jnp.concatenate([x1 * cos - x2 * sin, x2 * cos + x1 * sin], axis=-1).astype(x.dtype)

def to_chunks(t):
    b, h, s, d = t.shape
    return t.astype(jnp.float32).reshape(b, h, s // CHUNK, CHUNK, d)

def scan_chunk_states(kv, decay):
    decay = jnp.broadcast_to(decay, kv.shape)

    def step(state, inp):
        kv_n, d_n = inp
        return d_n * state + kv_n, state

    init = jnp.zeros(kv.shape[:2] + kv.shape[3:], kv.dtype)
    _, prev = lax.scan(step, init, (jnp.moveaxis(kv, 2, 0), jnp.moveaxis(decay, 2, 0)))
    return jnp.moveaxis(prev, 0, 2)

def gla_chunked(q, k, v, log_a):
    b, h, s, _ = q.shape
    q, k, v, log_a = to_chunks(q), to_chunks(k), to_chunks(v), to_chunks(log_a)
    g = jnp.cumsum(log_a, axis=3)
    g_last = g[:, :, :, -1:, :]
    ref = 0.5 * g_last
    causal = jnp.tril(jnp.ones((CHUNK, CHUNK), dtype=bool))
    scores = jnp.einsum('bhnid,bhnjd->bhnij', q * jnp.exp(g - ref), k * jnp.exp(ref - g))
    scores = jnp.where(causal, scores, 0.0)
    o_intra = jnp.einsum('bhnij,bhnje->bhnie', scores, v)
    kv = jnp.einsum('bhncd,bhnce->bhnde', k * jnp.exp(g_last - g), v)
    prev = scan_chunk_states(kv, jnp.exp(g_last[:, :, :, 0, :])[..., None])
    o_inter = jnp.einsum('bhncd,bhnde->bhnce', q * jnp.exp(g), prev)
    return (o_intra + o_inter).reshape(b, h, s, -1)

def retention_chunked(q, k, v, log_gamma):
    b, h, s, _ = q.shape
    q, k, v = to_chunks(q), to_chunks(k), to_chunks(v)
    idx = jnp.arange(CHUNK, dtype=jnp.float32)
    diff = idx[:, None] - idx[None, :]
    lg = log_gamma[:, None, None]
    decay_mask = jnp.where(diff >= 0, jnp.exp(lg * jnp.maximum(diff, 0.0)), 0.0)
    scores = jnp.einsum('bhnid,bhnjd->bhnij', q, k) * decay_mask[None, :, None]
    o_intra = jnp.einsum('bhnij,bhnje->bhnie', scores, v)
    q_dec = jnp.exp(log_gamma[:, None] * (idx + 1.0))
    k_dec = jnp.exp(log_gamma[:, None] * (CHUNK - 1.0 - idx))
    kv = jnp.einsum('bhncd,bhnce->bhnde', k * k_dec[None, :, None, :, None], v)
    prev = scan_chunk_states(kv, jnp.exp(log_gamma * CHUNK)[None, :, None, None, None])
    o_inter = jnp.einsum('bhncd,bhnde->bhnce', q, prev) * q_dec[None, :, None, :, None]
    return (o_intra + o_inter).reshape(b, h, s, -1)

def even_mixer(xn, positions, log_gamma, w_in, gla_w_up, gla_b_up, gla_norm_w, ret_norm_w, w_out):
    split_at = np.cumsum(EVEN_SPLIT_SIZES)[:-1].tolist()
    qa, ka, va, ga, ra, qb, kb, vb, gb = jnp.split(xn @ w_in, split_at, axis=-1)
    log_a = jax.nn.log_sigmoid((ra @ gla_w_up + gla_b_up).astype(jnp.float32)) / GLA_GATE_NORM
    o_a = gla_chunked(to_heads(qa, GLA_HEADS) * GLA_DK ** -0.5, to_heads(ka, GLA_HEADS),
                      to_heads(va, GLA_HEADS), to_heads(log_a, GLA_HEADS))
    o_a = from_heads(rms_norm(o_a, gla_norm_w)).astype(xn.dtype) * jax.nn.silu(ga)
    qb = rotary(to_heads(qb, RET_HEADS), positions)
    kb = rotary(to_heads(kb, RET_HEADS), positions) * RET_DK ** -0.5
    o_b = retention_chunked(qb, kb, to_heads(vb, RET_HEADS), log_gamma)
    o_b = (from_heads(group_norm(o_b)) * ret_norm_w).astype(xn.dtype) * jax.nn.silu(gb)
    return jnp.concatenate([o_a, o_b], axis=-1) @ w_out

def pool_mixer(u, pool_w, pool_scale):
    b, s, _ = u.shape
    ug = u.reshape(b, s, POOL_GROUPS, POOL_GROUP_WIDTH).astype(jnp.float32)
    cs = jnp.cumsum(ug, axis=1)
    t = jnp.arange(s)
    outs = []
    for g, win in enumerate(POOL_WINDOWS):
        c_g = cs[:, :, g]
        lagged = jnp.pad(c_g, ((0, 0), (win, 0), (0, 0)))[:, :s]
        count = jnp.minimum(t + 1, win).astype(jnp.float32)[None, :, None]
        outs.append((c_g - lagged) / count - ug[:, :, g])
    pooled = jnp.stack(outs, axis=2).astype(u.dtype)
    mixed = jnp.einsum('bsgc,gcd->bsgd', pooled, pool_w)
    return mixed.reshape(b, s, POOL_WIDTH) * pool_scale

def s5_mixer(u, a_re, a_im, log_dt, b_re, b_im, c_re, c_im, d_skip, w_glu, b_glu):
    b, s, _ = u.shape
    ug = u.reshape(b, s, S5_GROUPS, S5_H).astype(jnp.float32)
    dt = jnp.exp(log_dt.astype(jnp.float32))[:, None]
    a_re = a_re.astype(jnp.float32)
    a_im = a_im.astype(jnp.float32)
    mag = jnp.exp(a_re * dt)
    abar_re, abar_im = mag * jnp.cos(a_im * dt), mag * jnp.sin(a_im * dt)
    den = a_re * a_re + a_im * a_im
    nr, ni = abar_re - 1.0, abar_im
    coef_re = (nr * a_re + ni * a_im) / den
    coef_im = (ni * a_re - nr * a_im) / den
    bbar_re = coef_re[..., None] * b_re - coef_im[..., None] * b_im
    bbar_im = coef_re[..., None] * b_im + coef_im[..., None] * b_re
    bu_re = jnp.einsum('bsgh,gph->bsgp', ug, bbar_re)
    bu_im = jnp.einsum('bsgh,gph->bsgp', ug, bbar_im)
    lam_re = jnp.broadcast_to(abar_re, (1, s) + abar_re.shape)
    lam_im = jnp.broadcast_to(abar_im, (1, s) + abar_im.shape)

    def combine(e1, e2):
        a1r, a1i, b1r, b1i = e1
        a2r, a2i, b2r, b2i = e2
        return (a2r * a1r - a2i * a1i, a2r * a1i + a2i * a1r,
                a2r * b1r - a2i * b1i + b2r, a2r * b1i + a2i * b1r + b2i)

    _, _, x_re, x_im = lax.associative_scan(combine, (lam_re, lam_im, bu_re, bu_im), axis=1)
    y = (jnp.einsum('bsgp,ghp->bsgh', x_re, c_re) - jnp.einsum('bsgp,ghp->bsgh', x_im, c_im)
         + d_skip * ug)
    z = jax.nn.gelu(y.reshape(b, s, S5_WIDTH).astype(u.dtype), approximate=False)
    return z * jax.nn.sigmoid(z @ w_glu + b_glu)

def odd_mixer(xn, w_in, pool_w, pool_scale, a_re, a_im, log_dt, b_re, b_im, c_re, c_im, d_skip, w_glu, b_glu, w_out):
    u_c, u_d = jnp.split(xn @ w_in, [POOL_WIDTH], axis=-1)
    y_c = pool_mixer(u_c, pool_w, pool_scale)
    y_d = s5_mixer(u_d, a_re, a_im, log_dt, b_re, b_im, c_re, c_im, d_skip, w_glu, b_glu)
    return jnp.concatenate([y_c, y_d], axis=-1) @ w_out

def peer(xn, w_q, sub_keys, u_tab, v_tab):
    b, s, d = xn.shape
    t = b * s
    xf = xn.reshape(t, d)
    q = (xf @ w_q).reshape(t, PEER_HEADS, 2, PEER_DKEY // 2)
    scores = jnp.einsum('thpc,hpkc->thpk', q, sub_keys).astype(jnp.float32)
    s_top, i_top = lax.top_k(scores, PEER_TOPK)
    cand = (s_top[:, :, 0, :, None] + s_top[:, :, 1, None, :]).reshape(t, PEER_HEADS, PEER_TOPK * PEER_TOPK)
    s_best, flat = lax.top_k(cand, PEER_TOPK)
    e_a = jnp.take_along_axis(i_top[:, :, 0], flat // PEER_TOPK, axis=-1)
    e_b = jnp.take_along_axis(i_top[:, :, 1], flat % PEER_TOPK, axis=-1)
    n_blk = t // PEER_BLOCK
    experts = (e_a * PEER_NKEYS + e_b).reshape(n_blk, PEER_BLOCK, PEER_HEADS * PEER_TOPK)
    gates = jax.nn.softmax(s_best, axis=-1).astype(xn.dtype).reshape(n_blk, PEER_BLOCK, PEER_HEADS * PEER_TOPK)

    def expert_block(args):
        x_blk, e_blk, g_blk = args
        u_sel = jnp.take(u_tab, e_blk, axis=0)
        hid = jax.nn.gelu(jnp.einsum('tkd,td->tk', u_sel, x_blk), approximate=False)
        return jnp.einsum('tk,tkd->td', g_blk * hid, jnp.take(v_tab, e_blk, axis=0))

    out = lax.map(expert_block, (xf.reshape(n_blk, PEER_BLOCK, d), experts, gates))
    return out.reshape(b, s, d)

def setup_inputs(seed: int = 0) -> dict:
    key = jax.random.key(seed)
    ks = iter(jax.random.split(key, 48))
    f32 = jnp.float32

    def nrm(shape, scale):
        return jax.random.normal(next(ks), shape, f32) * scale

    def gain(shape):
        return 1.0 + nrm(shape, 0.02)

    x = nrm((BATCH, SEQ, D_MODEL), 1.0)
    p = nrm((DEPTH, BATCH, SEQ, PLE_DIM), 1.0)
    positions = jnp.arange(SEQ, dtype=jnp.int32)
    norm_mix_w = gain((DEPTH, D_MODEL))
    norm_ffn_w = gain((DEPTH, D_MODEL))
    norm_ple_w = gain((DEPTH, D_MODEL))
    final_norm_w = gain((D_MODEL,))
    ev_w_in = nrm((N_EVEN, D_MODEL, EVEN_PROJ), D_MODEL ** -0.5)
    ev_gla_w_up = nrm((N_EVEN, GLA_GATE_RANK, GLA_HEADS * GLA_DK), GLA_GATE_RANK ** -0.5)
    ev_gla_b_up = nrm((N_EVEN, GLA_HEADS * GLA_DK), 0.1)
    ev_gla_norm_w = gain((N_EVEN, GLA_DV))
    ev_ret_norm_w = gain((N_EVEN, RET_HEADS * RET_DV))
    ev_w_out = nrm((N_EVEN, MIX_WIDTH, D_MODEL), MIX_WIDTH ** -0.5)
    od_w_in = nrm((N_ODD, D_MODEL, MIX_WIDTH), D_MODEL ** -0.5)
    od_pool_w = nrm((N_ODD, POOL_GROUPS, POOL_GROUP_WIDTH, POOL_GROUP_WIDTH), POOL_GROUP_WIDTH ** -0.5)
    od_pool_scale = 1.0 + nrm((N_ODD, POOL_WIDTH), 0.1)
    od_s5_a_re = -0.5 + nrm((N_ODD, S5_GROUPS, S5_P), 0.01)
    od_s5_a_im = math.pi * jnp.arange(S5_P, dtype=f32) + nrm((N_ODD, S5_GROUPS, S5_P), 0.01)
    od_s5_log_dt = jax.random.uniform(next(ks), (N_ODD, S5_GROUPS), f32, math.log(DT_MIN), math.log(DT_MAX))
    od_s5_b_re = nrm((N_ODD, S5_GROUPS, S5_P, S5_H), (2.0 * S5_H) ** -0.5)
    od_s5_b_im = nrm((N_ODD, S5_GROUPS, S5_P, S5_H), (2.0 * S5_H) ** -0.5)
    od_s5_c_re = nrm((N_ODD, S5_GROUPS, S5_H, S5_P), (2.0 * S5_P) ** -0.5)
    od_s5_c_im = nrm((N_ODD, S5_GROUPS, S5_H, S5_P), (2.0 * S5_P) ** -0.5)
    od_s5_d = nrm((N_ODD, S5_GROUPS, S5_H), 1.0)
    od_s5_w_glu = nrm((N_ODD, S5_WIDTH, S5_WIDTH), S5_WIDTH ** -0.5)
    od_s5_b_glu = nrm((N_ODD, S5_WIDTH), 0.02)
    od_w_out = nrm((N_ODD, MIX_WIDTH, D_MODEL), MIX_WIDTH ** -0.5)
    peer_w_q = nrm((DEPTH, D_MODEL, PEER_HEADS * PEER_DKEY), D_MODEL ** -0.5)
    peer_sub_keys = nrm((DEPTH, PEER_HEADS, 2, PEER_NKEYS, PEER_DKEY // 2), (PEER_DKEY // 2) ** -0.5)
    peer_u = nrm((DEPTH, PEER_EXPERTS, D_MODEL), D_MODEL ** -0.5)
    peer_v = nrm((DEPTH, PEER_EXPERTS, D_MODEL), PEER_HEADS ** -0.5)
    ple_w_proj = nrm((DEPTH, PLE_DIM, D_MODEL), PLE_DIM ** -0.5)
    ple_w_gate = nrm((DEPTH, D_MODEL, D_MODEL), D_MODEL ** -0.5)
    return {'x': x, 'p': p, 'positions': positions,
            'norm_mix_w': norm_mix_w, 'norm_ffn_w': norm_ffn_w, 'norm_ple_w': norm_ple_w,
            'final_norm_w': final_norm_w,
            'ev_w_in': ev_w_in, 'ev_gla_w_up': ev_gla_w_up, 'ev_gla_b_up': ev_gla_b_up,
            'ev_gla_norm_w': ev_gla_norm_w, 'ev_ret_norm_w': ev_ret_norm_w, 'ev_w_out': ev_w_out,
            'od_w_in': od_w_in, 'od_pool_w': od_pool_w, 'od_pool_scale': od_pool_scale,
            'od_s5_a_re': od_s5_a_re, 'od_s5_a_im': od_s5_a_im, 'od_s5_log_dt': od_s5_log_dt,
            'od_s5_b_re': od_s5_b_re, 'od_s5_b_im': od_s5_b_im,
            'od_s5_c_re': od_s5_c_re, 'od_s5_c_im': od_s5_c_im, 'od_s5_d': od_s5_d,
            'od_s5_w_glu': od_s5_w_glu, 'od_s5_b_glu': od_s5_b_glu, 'od_w_out': od_w_out,
            'peer_w_q': peer_w_q, 'peer_sub_keys': peer_sub_keys, 'peer_u': peer_u, 'peer_v': peer_v,
            'ple_w_proj': ple_w_proj, 'ple_w_gate': ple_w_gate}

def reference(x, p, positions, norm_mix_w, norm_ffn_w, norm_ple_w, final_norm_w,
              ev_w_in, ev_gla_w_up, ev_gla_b_up, ev_gla_norm_w, ev_ret_norm_w, ev_w_out,
              od_w_in, od_pool_w, od_pool_scale, od_s5_a_re, od_s5_a_im, od_s5_log_dt,
              od_s5_b_re, od_s5_b_im, od_s5_c_re, od_s5_c_im, od_s5_d, od_s5_w_glu, od_s5_b_glu, od_w_out,
              peer_w_q, peer_sub_keys, peer_u, peer_v, ple_w_proj, ple_w_gate):
    log_gamma = jnp.log(1.0 - 2.0 ** (-5.0 - jnp.arange(RET_HEADS, dtype=jnp.float32)))
    h = x
    for i in range(DEPTH):
        j = i // 2
        xn = rms_norm(h, norm_mix_w[i])
        if i % 2 == 0:
            mix = even_mixer(xn, positions, log_gamma, ev_w_in[j], ev_gla_w_up[j], ev_gla_b_up[j],
                             ev_gla_norm_w[j], ev_ret_norm_w[j], ev_w_out[j])
        else:
            mix = odd_mixer(xn, od_w_in[j], od_pool_w[j], od_pool_scale[j], od_s5_a_re[j], od_s5_a_im[j],
                            od_s5_log_dt[j], od_s5_b_re[j], od_s5_b_im[j], od_s5_c_re[j], od_s5_c_im[j],
                            od_s5_d[j], od_s5_w_glu[j], od_s5_b_glu[j], od_w_out[j])
        h = h + mix
        h = h + peer(rms_norm(h, norm_ffn_w[i]), peer_w_q[i], peer_sub_keys[i], peer_u[i], peer_v[i])
        gate = jax.nn.sigmoid(rms_norm(h, norm_ple_w[i]) @ ple_w_gate[i])
        h = h + (p[i] @ ple_w_proj[i]) * gate
    return rms_norm(h, final_norm_w)


_drawn_inputs = setup_inputs


def setup_inputs(seed=0):
    import zlib

    import numpy as np

    out = dict(_drawn_inputs(seed))
    spreads = {}
    factors = {'norm_ple_w': 184.516,
     'final_norm_w': 19.755,
     'ev_gla_norm_w': 7.378,
     'ev_ret_norm_w': 7.971,
     'od_s5_a_re': 64.0,
     'od_s5_a_im': 29.408,
     'od_s5_log_dt': 29.928,
     'od_s5_b_re': 37.224,
     'od_s5_b_im': 36.192,
     'od_s5_c_re': 36.832,
     'od_s5_c_im': 35.84,
     'od_s5_b_glu': 111.767,
     'norm_ffn_w': 8.535,
     'od_pool_scale': 3.721,
     'od_s5_w_glu': 3.439}
    for name, (base, spread) in spreads.items():
        noise = np.random.default_rng([zlib.crc32(name.encode()), seed]).standard_normal(out[name].shape)
        drawn = base * np.exp(spread * noise) if base else spread * noise
        out[name] = jnp.asarray(drawn.astype(out[name].dtype))
    for name, factor in factors.items():
        out[name] = (out[name] * factor).astype(out[name].dtype)
    return out
```

```python
from contextlib import ExitStack

import numpy as np

import concourse.bass as bass
from concourse import mybir

ALU = mybir.AluOpType
ACT = mybir.ActivationFunctionType
F32 = mybir.dt.float32
F32R = mybir.dt.float32r
I32 = mybir.dt.int32
U32 = mybir.dt.uint32
AX_X = mybir.AxisListType.X

P = 128
SEQ = 256
NB = SEQ // P
D = 1024
DC = D // P
DEPTH = 2
EPS = 1e-6
CHUNK = 64
HEADS = 8
HD = 64
PAIRS = HEADS // 2
GATE_RANK = 16
GATE_NORM = 16.0
NKEYS = 128
TOPK = 16
PH = 8
HP = 2 * PH
PLE = 256
S5_TILES = 16
AHEAD = 36
NG = SEQ // 4
WINDOWS = (2, 4, 8, 16)
TWO_PI = 2.0 * np.pi
ROUND = 1.5 * 2.0 ** 23
C1 = 6.28125
C2 = float(np.float32(TWO_PI - C1))
C3 = float(np.float32(TWO_PI - C1 - C2))
PI_LOW = 3.1415925
LOWEST = -3.4e38

OUTPUTS = []


def plan_outputs():
    def add(taker, *names):
        OUTPUTS.extend((n, taker) for n in names)

    def transposed(site):
        add("dve", *[f"xnT{site}.{i}" for i in range(4)])

    def peer(layer):
        add("act", *[f"q{layer}.{i}" for i in range(8)])
        add("act", *[f"scores{layer}.{i}" for i in range(8)])
        add("act", *[f"routes{layer}.{i}" for i in range(2)])

    def ple(layer):
        add("act", *[f"gate{layer}.{i}" for i in range(4)])
        add("dve", *[f"ple{layer}.{i}" for i in range(4)])

    OUTPUTS.clear()
    transposed(0)
    add("act", "qaT", "kaT", "raT")
    add("dve", "zT")
    for name in ("va", "ga", "qkb", "vb", "gb"):
        add("act", *[f"{name}.{B}" for B in range(NB)])
    add("act", "rqT", "rkT", "kgT", "sT.0", "sT.1")
    add("dve", "kv.0", "kv.1", "kv.2")
    add("act", *[f"o.{i}" for i in range(4)])
    add("act", *[f"oT.{i}" for i in range(4)])
    add("dve", *[f"mix0.{i}" for i in range(4)])
    transposed(1)
    peer(0)
    transposed(2)
    ple(0)
    transposed(3)
    add("act", "ucT.0", "ucT.1", "udT.0", "udT.1")
    add("act", "pmT.0", "pmT.1")
    for half in range(2):
        add("dve", *[f"bu.{8 * half + j}" for j in range(8)])
        add("dve", f"ys.{half}")
    add("act", "glu.0", "glu.1")
    add("dve", *[f"mix1.{i}" for i in range(4)])
    transposed(4)
    peer(1)
    transposed(5)
    ple(1)


plan_outputs()
NUMBER = {name: n for n, (name, _) in enumerate(OUTPUTS)}
RANK = {name: sum(t == taker for _, t in OUTPUTS[:n]) for n, (name, taker) in enumerate(OUTPUTS)}

CONST = {}


def constants():
    p = np.arange(P)
    lg = np.log(1.0 - 2.0 ** (-5.0 - np.arange(4)))
    j = p % CHUNK
    i = np.arange(CHUNK)
    scale = HD ** -0.5
    diff = i[None, None, :] - j[:, None, None]
    retmask = np.where(diff >= 0, np.exp(lg[None, :, None] * np.maximum(diff, 0)), 0.0) * scale
    head = 2 * np.arange(2)[None, :] + (p // HD)[:, None]
    qdec = np.exp(lg[head][:, :, None] * (i + 1.0))
    kdec = np.exp(lg[None, :] * (CHUNK - 1.0 - j[:, None])) * scale
    gend = np.exp(lg[head] * CHUNK)
    freq = np.float32(10000.0) ** (-np.arange(32, dtype=np.float32) / np.float32(32))
    starts = (np.arange(SEQ) % CHUNK != 0).astype(np.float32)
    t = np.arange(SEQ)
    parts = [
        ("ident", np.eye(P)), ("iota", np.tile(p, (P, 1))), ("iota16", np.tile(p[:16], (P, 1))),
        ("gend", gend), ("kdec", kdec), ("freq", np.tile(freq, (P, 1))),
        ("retmask", retmask.reshape(P, -1)), ("qdec", qdec.reshape(P, -1)), ("starts", np.tile(starts, (P, 1))),
        ("time", np.tile(t, (P, 1))),
    ]
    at = 0
    for name, a in parts:
        CONST[name] = (at, at + a.shape[1])
        at += a.shape[1]
    count = np.stack([1.0 / np.minimum(t + 1.0, w) for w in WINDOWS])
    return (np.concatenate([a for _, a in parts], axis=1).astype(np.float32),
            np.tile(count.reshape(1, -1), (P, 1)).astype(np.float32))


NCONST = constants()[0].shape[1]

COL = {}
for _name, _w in (("mix0", 8), ("ffn0", 8), ("ple0", 8), ("mix1", 8), ("ffn1", 8), ("ple1", 8), ("bup", 2),
                  ("pscale", 4), ("dskip", 4), ("bglu", 4), ("are", 16), ("aim", 16), ("ldt", 16)):
    _at = sum(w for _, w in COL.values())
    COL[_name] = (_at, _w)
NCOL = sum(w for _, w in COL.values())
SITES = ("mix0", "ffn0", "ple0", "mix1", "ffn1", "ple1")


def program(nc, consts, counts, cols, rows, pos, x, pT, w_even, w_ra, w_up, w_out0, w_odd, w_pool, s5_b, s5_c,
            w_glu, w_out1, w_q, keys, u_tab, v_tab, w_ple, w_gate, out):
    with ExitStack() as ctx:
        def sb(name, shape, dt=F32):
            return ctx.enter_context(nc.sbuf_tensor(name, shape, dt))

        def sem(name):
            return ctx.enter_context(nc.semaphore(name))

        banks = [ctx.enter_context(nc.psum_tensor(f"bank{i}", [P, 512], F32)) for i in range(8)]

        big = sb("big", [P, 32768])
        raw = sb("raw", [P, 4096])
        halves = sb("halves", [P, 9216], F32R)
        h = sb("h", [P, NB, D])
        xnT = sb("xnT", [P, DC, SEQ])
        cst = sb("cst", [P, NCONST])
        col = sb("col", [P, NCOL])
        posi = sb("posi", [P, NB], I32)
        routesT = sb("routesT", [P, 3, SEQ])
        small = sb("small", [P, 600])

        def C(name):
            a, b = CONST[name]
            return cst[:, a:b]

        def K(name, i=0, n=None):
            a, w = COL[name]
            return col[:, a + i:a + (i + n if n else w)]

        def region(base, a, n):
            return base[:, a:a + n]

        ident = C("ident")
        xs = region(big, 28672, 2048).rearrange("p (b f) -> p b f", b=NB)
        final_row = region(big, 20480, D)

        s_const = sem("const_loaded")
        s_x = sem("x_loaded")
        s_row = sem("rows_loaded")
        s_up = sem("wup_loaded")
        s_win = [sem(f"w_even_loaded{i}") for i in range(3)]
        s_wra = sem("w_ra_loaded")
        s_wout = sem("w_out_loaded")
        s_wq = sem("w_q_loaded")
        s_keys = sem("keys_loaded")
        s_ple = sem("ple_loaded")
        s_odd = sem("w_odd_loaded")
        s_s5 = sem("s5_loaded")
        s_late = sem("glu_pool_loaded")
        s_u = [sem(f"u_loaded{i}") for i in range(2)]
        s_v = [sem(f"v_loaded{i}") for i in range(2)]
        s_out = sem("out_stored")

        pe_out = sem("pe_output")
        taken = {"act": sem("act_took"), "dve": sem("dve_took")}
        v_step = sem("dve_step")
        a_step = sem("act_step")
        s_rows = sem("other_rows_done")
        s_var = sem("norm_var")
        s_rstd = sem("norm_rstd")
        s_xs = sem("xs_ready")
        s_log = sem("gate_abs_ready")
        s_loga = sem("gate_log_ready")
        s_gd = sem("gate_sums_ready")
        s_ge = sem("gate_exp_ready")
        s_qt = sem("gla_qk_ready")
        s_rope_ang = sem("rope_angle_ready")
        s_rope_sin = sem("rope_sin_ready")
        s_rot = sem("rope_ready")
        s_ret = sem("ret_q_inter_ready")
        s_masked_v = sem("ret_scores_decayed")
        s_masked_p = sem("gla_scores_masked")
        s_cen = sem("heads_centred")
        s_sq = sem("heads_squared")
        s_hvar = sem("heads_var")
        s_hrstd = sem("heads_rstd")
        s_silu = sem("silu_ready")
        s_oready = sem("heads_out_ready")
        s_best = sem("best_minus_max")
        s_exp = sem("best_exp")
        s_route = sem("routes_ready")
        s_ab = sem("onehot_ready")
        s_wps = sem("w_psum_ready")
        s_wsb = sem("w_ready")
        s_wmul = sem("w_times_hidden")
        s_xh = sem("x_high_ready")
        s_xl = sem("x_low_ready")
        s_uh = sem("u_high_ready")
        s_ul = sem("u_low_ready")
        s_uused = sem("u_halves_used")
        s_vh = sem("v_high_ready")
        s_vl = sem("v_low_ready")
        s_vused = sem("v_halves_used")
        s_gelu = sem("gelu_ready")
        s_pm = sem("gated_product")
        s_pf = sem("gated_high_ready")
        s_p = sem("gated_ready")
        s_par_a = sem("s5_par_act")
        s_par_v = sem("s5_par_dve")
        s_ang = sem("s5_angle_ready")
        s_sin = sem("s5_sin_ready")
        s_c = sem("s5_c_ready")
        s_pool = sem("pooled_ready")
        s_xst = sem("s5_states_ready")
        s_xused = sem("s5_states_used")
        s_z = sem("s5_z_ready")
        s_mt = sem("s5_out_ready")
        s_fin = sem("final_ready")

        count = {}

        def done(eng, ins, s):
            count[s] = count.get(s, 0) + 1
            ins.then_inc(s, 1)
            eng.wait_ge(s, count[s])

        def took(eng, ins, who):
            done(eng, ins, taken[who])

        def output(pe, name):
            n = NUMBER[name]
            if n >= 8:
                before, taker = OUTPUTS[n - 8]
                pe.wait_ge(taken[taker], RANK[before] + 1)
            return banks[n % 8]

        def arrive(eng, name):
            eng.wait_ge(pe_out, NUMBER[name] + 1)
            return banks[NUMBER[name] % 8]

        def ready(eng, name):
            eng.wait_ge(taken[dict(OUTPUTS)[name]], RANK[name] + 1)

        wring = [region(big, 4096 * i, 4096).rearrange("p (c n) -> p c n", c=DC) for i in range(3)]
        at = [12288]

        def place(n):
            a = at[0]
            at[0] += n
            assert at[0] <= 32768, at[0]
            return region(big, a, n)

        mix_row = place(1024)
        wup = place(256)[0:GATE_RANK, :]
        wra = place(128).rearrange("p (c n) -> p c n", c=DC)
        QT = place(1024).rearrange("p (q t) -> p q t", q=PAIRS)
        KT = place(1024).rearrange("p (q t) -> p q t", q=PAIRS)
        QI = place(1024).rearrange("p (q t) -> p q t", q=PAIRS)
        KI = place(1024).rearrange("p (b f) -> p b f", b=NB)
        Vf = place(2048)
        V = Vf.rearrange("p (b f) -> p b f", b=NB)
        MT = Vf.rearrange("p (c t) -> p c t", c=DC)
        SGf = place(2048)
        SG = SGf.rearrange("p (b f) -> p b f", b=NB)
        qrf = place(2048)
        QKB = qrf[:, 0:1024].rearrange("p (b f) -> p b f", b=NB)
        ROT = qrf[:, 1024:2048].rearrange("p (b f) -> p b f", b=NB)
        SQ = qrf
        ST = place(1024).rearrange("p (b h i) -> p b h i", b=NB, h=HEADS)
        STATE = place(1536).rearrange("p (n q e) -> p n q e", n=3, q=PAIRS)
        Of = place(2048)
        O = Of.rearrange("p (b f) -> p b f", b=NB)
        gz, ge, gl, gg, gd = [place(512) for _ in range(5)]
        raT = place(256)[0:GATE_RANK, :]
        trig = [place(64) for _ in range(6)]
        qraw = place(512).rearrange("p (q t) -> p q t", q=2)
        kraw = place(512).rearrange("p (q t) -> p q t", q=2)
        wout0 = [w.rearrange("p c n -> p (c n)").rearrange("p (c n) -> p c n", c=4) for w in wring[0:2]]

        wout1 = [raw[:, :].rearrange("p (c n) -> p c n", c=4), region(big, 8192, 4096).rearrange("p (c n) -> p c n", c=4)]
        wodd = region(big, 0, 8192).rearrange("p (c n) -> p c n", c=DC)
        wglu = region(big, 0, 2048).rearrange("p (c n) -> p c n", c=4)
        wpool = region(big, 2048, 512).rearrange("p (g n) -> p g n", g=4)
        SGL = region(big, 2560, 1024).rearrange("p (c t) -> p c t", c=4)
        PM = region(big, 3584, 1024).rearrange("p (c t) -> p c t", c=4)
        P1 = region(big, 4608, 1024).rearrange("p (c t) -> p c t", c=4)
        P2 = region(big, 5632, 1024).rearrange("p (c t) -> p c t", c=4)
        INV = region(big, 6656, 1024).rearrange("p (c t) -> p c t", c=4)
        cosE = region(big, 8192, 2048).rearrange("p (j t) -> p j t", j=8)
        sinE = region(big, 10240, 2048).rearrange("p (j t) -> p j t", j=8)
        VS = region(big, 12288, 4096)
        YS = region(big, 16384, 4096)
        WS = region(big, 20480, 4096)
        s5b = region(big, 24576, 1024).rearrange("p (q r n) -> p q r n", q=4, r=2)
        s5c = region(big, 25600, 1024).rearrange("p (r j n) -> p r j n", r=2, j=S5_TILES)
        s5d = region(big, 26624, 1024).rearrange("p (r j n) -> p r j n", r=2, j=S5_TILES)
        UC = region(big, 27648, 1024).rearrange("p (c t) -> p c t", c=4)
        UD = region(big, 28672, 1024).rearrange("p (c t) -> p c t", c=4)
        MT1 = region(big, 29696, 2048).rearrange("p (c t) -> p c t", c=DC)
        Z = region(big, 31744, 1024).rearrange("p (c t) -> p c t", c=4)
        YD = SGL

        wq = region(big, 0, 16384).rearrange("p (c n) -> p c n", c=DC)
        qT = region(big, 16384, 4096).rearrange("p (g t) -> p g t", g=HP)
        SC = region(big, 20480, 4096).rearrange("p (b g k) -> p b g k", b=NB, g=HP)
        keysT = region(big, 24576, 2048).rearrange("p (g k) -> p g k", g=HP)
        CAND = region(big, 26624, 2048).rearrange("p (h c) -> p h c", h=PH)
        EQ = region(big, 28672, 2048)
        tk = [region(big, 30720 + 256 * i, 256) for i in range(8)]
        W = big[:, :].rearrange("p (b t) -> p b t", t=SEQ)
        OH = xnT[:, :, :].rearrange("p c t -> p (c t)").rearrange("p (b w t k) -> p b w t k", b=2, w=2, t=4)
        PF = [xnT[:, i, :] for i in range(2)]
        xh = halves[:, 0:2048].rearrange("p (c t) -> p c t", c=DC)
        xl = halves[:, 2048:4096].rearrange("p (c t) -> p c t", c=DC)
        uh, ul, vh, vl = [[halves[:, 4096 + 1024 * k + 512 * i:4608 + 1024 * k + 512 * i] for i in range(2)]
                          for k in range(4)]
        ph, pl = [[halves[:, 8192 + 512 * k + 256 * i:8448 + 512 * k + 256 * i] for i in range(2)] for k in range(2)]
        uraw = [raw[:, 1024 * i:1024 * i + 1024] for i in range(2)]
        vraw = [raw[:, 2048 + 1024 * i:3072 + 1024 * i] for i in range(2)]

        wgate = region(big, 0, 8192).rearrange("p (c n) -> p c n", c=DC)
        wple = region(big, 8192, 2048).rearrange("p (c n) -> p c n", c=2)
        pTs = region(big, 10240, 512).rearrange("p (c t) -> p c t", c=2)
        GT = region(big, 12288, 2048).rearrange("p (b f) -> p b f", b=NB)

        def sm(i, n):
            return small[:, i:i + n]

        def over_b(eng, body, start, stop):
            pairs = (stop - start) // 2
            with eng.Fori(0, pairs) as it:
                for k in range(2):
                    body(it * 2 + (start + k), it + (start + k) // 2, (start + k) % 2)
            if (stop - start) % 2:
                body(stop - 1, (stop - 1) // 2, (stop - 1) % 2)

        def after(eng, s, value):
            if not isinstance(value, int) or value > 0:
                eng.wait_ge(s, value)

        block = ctx.enter_context(nc.Block())

        @block.sync
        def _(sp):
            sp.dma_start(h[:, :, :], x).then_inc(s_x, 16)
            sp.dma_start(cst[:, :], consts).then_inc(s_const, 16)
            sp.dma_start(col[:, :], cols).then_inc(s_const, 16)
            sp.dma_start(posi[:, :], pos).then_inc(s_const, 16)
            sp.dma_start(wra, w_ra).then_inc(s_wra, 16)
            sp.dma_start(wup, w_up).then_inc(s_up, 16)
            for g in range(3):
                sp.dma_start(wring[g], w_even[g]).then_inc(s_win[g], 16)
            sp.dma_start(mix_row, rows[:, 0:D]).then_inc(s_row, 16)
            for g in range(3, 6):
                sp.wait_ge(pe_out, NUMBER[("kaT", "va.1", "ga.1")[g - 3]] + 1)
                sp.dma_start(wring[g % 3], w_even[g]).then_inc(s_win[g % 3], 16)
            for i in range(2):
                sp.wait_ge(pe_out, NUMBER[("qkb.1", "vb.1")[i]] + 1)
                sp.dma_start(wout0[i], w_out0[:, 4 * i:4 * i + 4, :]).then_inc(s_wout, 16)
            for layer in range(DEPTH):
                if layer:
                    sp.wait_ge(taken["dve"], RANK["ple0.3"] + 1)
                    sp.dma_start(wodd, w_odd).then_inc(s_odd, 16)
                    sp.dma_start(s5b, s5_b).then_inc(s_s5, 16)
                    sp.dma_start(s5c, s5_c).then_inc(s_s5, 16)
                    sp.dma_start(wout1[0], w_out1[:, 0:4, :]).then_inc(s_wout, 16)
                    sp.wait_ge(pe_out, NUMBER["udT.1"] + 1)
                    sp.dma_start(wglu, w_glu).then_inc(s_late, 16)
                    sp.dma_start(wpool, w_pool).then_inc(s_late, 16)
                    sp.dma_start(INV, counts).then_inc(s_late, 16)
                    sp.wait_ge(s_xst, 2)
                    sp.dma_start(wout1[1], w_out1[:, 4:8, :]).then_inc(s_wout, 16)
                sp.wait_ge(pe_out, NUMBER[f"mix{layer}.3"] + 1)
                for q in range(2):
                    sp.dma_start(wq[:, 4 * q:4 * q + 4, :], w_q[layer, :, 4 * q:4 * q + 4, :]).then_inc(s_wq, 16)
                sp.dma_start(keysT, keys[layer]).then_inc(s_keys, 16)
                for s in range(2):
                    sp.dma_start(uraw[s], u_tab[layer, s]).then_inc(s_u[s], 16)
                    sp.dma_start(vraw[s], v_tab[layer, s]).then_inc(s_v[s], 16)
                b0 = NKEYS * layer

                def load_u(b, s):
                    sp.wait_ge(s_ul, b * 2 + (2 * b0 - 2))
                    sp.dma_start(uraw[s], u_tab[layer, bass.ds(b, 1)].rearrange("o p n -> p (o n)")).then_inc(s_u[s], 16)

                def load_v(b, s):
                    sp.wait_ge(s_vl, b * 2 + (2 * b0 - 2))
                    sp.dma_start(vraw[s], v_tab[layer, bass.ds(b, 1)].rearrange("o p n -> p (o n)")).then_inc(s_v[s], 16)

                def load_both(b, h_, s):
                    load_u(b + 1, 1 - s)
                    load_v(b, s)

                over_b(sp, lambda b, h_, s: load_u(b, s), 2, AHEAD + 2)
                over_b(sp, lambda b, h_, s: load_v(b, s), 2, AHEAD + 1)
                over_b(sp, load_both, AHEAD + 1, NKEYS - 1)
                load_v(NKEYS - 1, 1)
                sp.wait_ge(s_p, NKEYS * (layer + 1))
                sp.dma_start(wgate, w_gate[layer]).then_inc(s_ple, 16)
                sp.dma_start(wple, w_ple[layer]).then_inc(s_ple, 16)
                sp.dma_start(pTs, pT[layer]).then_inc(s_ple, 16)
            sp.dma_start(final_row, rows[:, D:2 * D]).then_inc(s_row, 16)
            sp.wait_ge(s_fin, 2)
            sp.dma_start(out, xs).then_inc(s_out, 16)
            sp.wait_ge(s_out, 16)

        @block.tensor
        def _(pe):
            def emit(name, ins):
                ins.then_inc(pe_out, 1)

            def transpose_norm(site):
                for i in range(4):
                    B, c0 = i // 2, 4 * (i % 2)
                    pe.wait_ge(s_xs, 2 * site + B + 1)
                    o = output(pe, f"xnT{site}.{i}")
                    for c in range(4):
                        last = pe.transpose(o[:, c * P:(c + 1) * P], xs[:, B, (c0 + c) * P:(c0 + c + 1) * P], ident)
                    emit(f"xnT{site}.{i}", last)
                ready(pe, f"xnT{site}.3")

            def product(o, pairs):
                for i, (a, b) in enumerate(pairs):
                    last = pe.matmul(o, a, b, start=(i == 0), stop=(i == len(pairs) - 1))
                return last

            def tokens_by(name, lhs, rhs, n=DC):
                for i in range(4):
                    B, hf = i // 2, i % 2
                    o = output(pe, f"{name}.{i}")
                    emit(name, product(o[:, :], [(lhs[:, c, B * P:(B + 1) * P], rhs(c)[:, 512 * hf:512 * hf + 512])
                                                 for c in range(n)]))

            pe.wait_ge(s_const, 48)
            transpose_norm(0)
            pe.wait_ge(s_win[0], 16)
            for m, name in enumerate(("qaT", "kaT")):
                o = output(pe, name)
                for q in range(2):
                    f = 256 * m + P * q
                    last = product(o[:, 256 * q:256 * q + 256], [(wring[0][:, c, f:f + P], xnT[:, c, :]) for c in range(DC)])
                emit(name, last)
            pe.wait_ge(s_wra, 16)
            o = output(pe, "raT")
            emit("raT", product(o[0:GATE_RANK, 0:SEQ], [(wra[:, c, :], xnT[:, c, :]) for c in range(DC)]))
            pe.wait_ge(s_up, 16)
            ready(pe, "raT")
            o = output(pe, "zT")
            for q in range(2):
                last = pe.matmul(o[:, 256 * q:256 * q + 256], wup[:, P * q:P * q + P], raT, start=True, stop=True)
            emit("zT", last)
            for g, name in enumerate(("va", "ga", "qkb", "vb", "gb"), start=1):
                pe.wait_ge(s_win[g % 3], 16 * (g // 3 + 1))
                for B in range(NB):
                    o = output(pe, f"{name}.{B}")
                    last = product(o[:, :], [(xnT[:, c, B * P:(B + 1) * P], wring[g % 3][:, c, :]) for c in range(DC)])
                    emit(name, last)
            pe.wait_ge(s_rot, 2)
            for m, name in enumerate(("rqT", "rkT")):
                o = output(pe, name)
                for q in range(2):
                    for B in range(NB):
                        f = 256 * m + P * q
                        last = pe.transpose(o[:, 256 * q + P * B:256 * q + P * B + P], ROT[:, B, f:f + P], ident)
                emit(name, last)
            pe.wait_ge(s_qt, 4)
            o = output(pe, "kgT")
            for B in range(NB):
                for q in range(2):
                    last = pe.transpose(o[:, 256 * B + P * q:256 * B + P * q + P], kraw[:, q, B * P:(B + 1) * P], ident)
            emit("kgT", last)
            ready(pe, "rkT")
            for B in range(NB):
                o = output(pe, f"sT.{B}")
                for odd in range(2):
                    for p in range(2):
                        for hh in range(odd, HEADS, 2):
                            r, t0 = HD * odd, B * P + CHUNK * p
                            last = pe.matmul(o[HD * p:HD * p + HD, 64 * hh:64 * hh + 64],
                                             KT[r:r + HD, hh // 2, t0:t0 + CHUNK], QT[r:r + HD, hh // 2, t0:t0 + CHUNK],
                                             start=True, stop=True)
                    if not odd:
                        done(pe, last, s_rows)
                emit("sT", last)
            ready(pe, "kgT")
            pe.wait_ge(s_ret, 3)
            for n in range(3):
                o = output(pe, f"kv.{n}")
                B, r = n // 2, CHUNK * (n % 2)
                for hh in range(HEADS):
                    q, d0 = hh // 2, HD * (hh % 2)
                    last = pe.matmul(o[d0:d0 + HD, P * q:P * q + P], KI[r:r + CHUNK, B, HD * hh:HD * hh + HD],
                                     V[r:r + CHUNK, B, P * hh:P * hh + P], start=True, stop=True)
                emit("kv", last)
            pe.wait_ge(s_masked_v, 2)
            pe.wait_ge(s_masked_p, 4)
            ready(pe, "kv.2")
            for i in range(4):
                B, hf = i // 2, i % 2
                o = output(pe, f"o.{i}")
                heads = range(4 * hf, 4 * hf + 4)

                def dst(p, hh):
                    return o[CHUNK * p:CHUNK * p + CHUNK, P * (hh % 4):P * (hh % 4) + P]

                for p in range(2):
                    for hh in heads:
                        last = pe.matmul(dst(p, hh), ST[CHUNK * p:CHUNK * p + CHUNK, B, hh, :],
                                         V[CHUNK * p:CHUNK * p + CHUNK, B, P * hh:P * hh + P],
                                         start=(hh == heads[0]), stop=False, skip_group_check=True)
                for other in range(2):
                    if other:
                        done(pe, last, s_rows)
                    for p in range(2):
                        n = 2 * B + p
                        for hh in heads:
                            if n and (hh + p) % 2 == other:
                                r, t0 = HD * (hh % 2), CHUNK * n
                                last = pe.matmul(dst(p, hh), QI[r:r + HD, hh // 2, t0:t0 + CHUNK],
                                                 STATE[r:r + HD, n - 1, hh // 2, :], start=False, stop=True,
                                                 skip_group_check=True)
                emit("o", last)
            pe.wait_ge(s_oready, 1)
            for i in range(4):
                B, c0 = i // 2, 4 * (i % 2)
                o = output(pe, f"oT.{i}")
                for c in range(4):
                    last = pe.transpose(o[:, c * P:(c + 1) * P], O[:, B, (c0 + c) * P:(c0 + c + 1) * P], ident)
                emit("oT", last)
            ready(pe, "oT.3")
            pe.wait_ge(s_wout, 32)
            tokens_by("mix0", MT, lambda c: wout0[c // 4][:, c % 4, :])

            for layer in range(DEPTH):
                if layer:
                    transpose_norm(3)
                    pe.wait_ge(s_odd, 16)
                    for m in range(4):
                        name = ("ucT.0", "ucT.1", "udT.0", "udT.1")[m]
                        o = output(pe, name)
                        for q in range(2):
                            f = 256 * m + P * q
                            last = product(o[:, 256 * q:256 * q + 256], [(wodd[:, c, f:f + P], xnT[:, c, :]) for c in range(DC)])
                        emit(name, last)
                    pe.wait_ge(s_late, 48)
                    pe.wait_ge(s_pool, 1)
                    for m in range(2):
                        o = output(pe, f"pmT.{m}")
                        for q in range(2):
                            last = pe.matmul(o[:, 256 * q:256 * q + 256], wpool[:, 2 * m + q, :], PM[:, 2 * m + q, :],
                                             start=True, stop=True)
                        emit("pmT", last)
                    pe.wait_ge(s_s5, 32)
                    ready(pe, "udT.1")
                    for half in range(2):
                        for j in range(8 * half, 8 * half + 8):
                            o = output(pe, f"bu.{j}")
                            r, q = 32 * (j % 4), j // 4
                            for ri in range(2):
                                last = pe.matmul(o[:, 256 * ri:256 * ri + 256], s5b[r:r + 32, q, ri, :], UD[r:r + 32, q, :],
                                                 start=True, stop=True)
                            emit("bu", last)
                        pe.wait_ge(s_xst, half + 1)
                        pe.wait_ge(s_c, 1)
                        o = output(pe, f"ys.{half}")
                        xst = VS.rearrange("p (r j t) -> p r j t", r=2, j=8)
                        for q in range(2):
                            for jj in range(4):
                                j = 4 * q + jj
                                for ri in range(2):
                                    last = pe.matmul(o[32 * jj:32 * jj + 32, 256 * q:256 * q + 256],
                                                     s5d[:, ri, 8 * half + j, :], xst[:, ri, j, :],
                                                     start=(ri == 0), stop=(ri == 1))
                        emit("ys", last)
                    pe.wait_ge(s_z, 1)
                    for m in range(2):
                        o = output(pe, f"glu.{m}")
                        for q in range(2):
                            f = 256 * m + P * q
                            last = product(o[:, 256 * q:256 * q + 256], [(wglu[:, c, f:f + P], Z[:, c, :]) for c in range(4)])
                        emit("glu", last)
                    ready(pe, "pmT.1")
                    pe.wait_ge(s_mt, 1)
                    pe.wait_ge(s_wout, 64)
                    tokens_by("mix1", MT1, lambda c: wout1[c // 4][:, c % 4, :])

                transpose_norm(1 + 3 * layer)
                pe.wait_ge(s_wq, 32 * (layer + 1))
                for m in range(8):
                    o = output(pe, f"q{layer}.{m}")
                    for q in range(2):
                        f = 256 * m + P * q
                        last = product(o[:, 256 * q:256 * q + 256], [(wq[:, c, f:f + P], xnT[:, c, :]) for c in range(DC)])
                    emit("q", last)
                pe.wait_ge(s_keys, 16 * (layer + 1))
                ready(pe, f"q{layer}.7")
                for i in range(8):
                    B, g0 = i // 4, 4 * (i % 4)
                    o = output(pe, f"scores{layer}.{i}")
                    for g in range(4):
                        last = pe.matmul(o[:, P * g:P * g + P], qT[:, g0 + g, B * P:(B + 1) * P], keysT[:, g0 + g, :],
                                         start=True, stop=True)
                    emit("scores", last)
                b0 = NKEYS * layer

                def hidden(b, s, bank_free):
                    after(pe, bank_free, b + (b0 - 1))
                    for half in range(2):
                        pe.wait_ge(s_ul, b * 2 + (2 * b0 + half + 1))
                        for c in range(4):
                            u_hi, u_lo = [u[half][:, c * P:(c + 1) * P] for u in (uh, ul)]
                            x_hi, x_lo = xh[:, 4 * half + c, :], xl[:, 4 * half + c, :]
                            pe.matmul(banks[s][:, 0:SEQ], u_lo, x_hi, start=(half == 0 and c == 0), stop=False)
                            pe.matmul(banks[s][:, 0:SEQ], u_hi, x_lo, start=False, stop=False)
                            last = pe.matmul(banks[s][:, 0:SEQ], u_hi, x_hi, start=False, stop=(half == 1 and c == 3))
                        last.then_inc(s_uused, 1)

                def gated(b, s, first=False, final=False):
                    pe.wait_ge(s_p, b + (b0 + 1))
                    for hf in range(2):
                        pe.wait_ge(s_vl, b * 2 + (2 * b0 + hf + 1))
                        for B in range(NB):
                            acc = banks[4 + 2 * B + hf][:, :]
                            p_hi, p_lo = [x[s][:, B * P:(B + 1) * P] for x in (ph, pl)]
                            pe.matmul(acc, p_lo, vh[hf], start=first, stop=False, skip_group_check=True)
                            pe.matmul(acc, p_hi, vl[hf], start=False, stop=False, skip_group_check=True)
                            last = pe.matmul(acc, p_hi, vh[hf], start=False, stop=final, skip_group_check=True)
                        last.then_inc(s_vused, 1)

                ready(pe, f"scores{layer}.7")
                pe.wait_ge(s_xl, layer + 1)
                for b in range(2):
                    hidden(b, b, s_gelu)
                over_b(pe, lambda b, h_, s: hidden(b, s, s_gelu), 2, AHEAD)
                pe.wait_ge(s_gelu, b0 + AHEAD)
                for B in range(NB):
                    pe.wait_ge(s_route, NB * layer + B + 1)
                    o = output(pe, f"routes{layer}.{B}")
                    for k in range(3):
                        last = pe.transpose(o[:, P * k:P * k + P], tk[5 + k][:, P * B:P * B + P], ident)
                    emit("routes", last)
                ready(pe, f"routes{layer}.1")

                def gate_group(g, k, first):
                    pe.wait_ge(s_ab, g + (NG * layer + 1))
                    if not first:
                        pe.wait_ge(s_wmul, g + (NG * layer - 3))
                    for t in range(4):
                        last = pe.matmul(banks[k][:, P * t:P * t + P], OH[:, k % 2, 0, t, :], OH[:, k % 2, 1, t, :],
                                         start=True, stop=True)
                    last.then_inc(s_wps, 1)

                for g in range(4):
                    gate_group(g, g, True)
                with pe.Fori(1, NG // 4) as it:
                    for k in range(4):
                        gate_group(it * 4 + k, k, False)
                pe.wait_ge(s_wmul, NG * (layer + 1))
                gated(0, 0, first=True)
                over_b(pe, lambda b, h_, s: gated(b, s), 1, AHEAD - 1)

                def both(b, h_, s):
                    hidden(b + 1, 1 - s, s_p)
                    gated(b, s)

                both(AHEAD - 1, None, (AHEAD - 1) % 2)
                over_b(pe, both, AHEAD, NKEYS - 1)
                gated(NKEYS - 1, 1, final=True)

                transpose_norm(2 + 3 * layer)
                pe.wait_ge(s_ple, 48 * (layer + 1))
                tokens_by(f"gate{layer}", xnT, lambda c: wgate[:, c, :])
                tokens_by(f"ple{layer}", pTs, lambda c: wple[:, c, :], n=2)

        @block.scalar
        def _(act):
            def step(ins):
                done(act, ins, a_step)

            def copy_out(name, dst, src=None, func=ACT.Copy, **kw):
                o = arrive(act, name)
                took(act, act.activation(dst, (o[:, :] if src is None else src(o)), func, **kw), "act")

            def norm_rstd(site):
                act.wait_ge(s_var, site + 1)
                done(act, act.activation(sm(4, 2), sm(2, 2), ACT.Sqrt), s_rstd)

            norm_rstd(0)
            act.wait_ge(s_rope_ang, 1)
            act.activation(trig[2], trig[0], ACT.Sin).then_inc(s_rope_sin, 1)
            act.activation(trig[3], trig[0], ACT.Sin, scale=0.5).then_inc(s_rope_sin, 1)
            copy_out("qaT", qraw.rearrange("p q t -> p (q t)"), scale=HD ** -0.5)
            copy_out("kaT", kraw.rearrange("p q t -> p (q t)"))
            copy_out("raT", raT, lambda o: o[0:GATE_RANK, 0:SEQ])
            act.wait_ge(s_log, 1)
            step(act.activation(ge, ge, ACT.Exp, scale=-1.0))
            done(act, act.activation(gl, ge, ACT.Ln, bias=1.0), s_loga)
            for B in range(NB):
                copy_out(f"va.{B}", V[:, B, 0:512])
            for B in range(NB):
                copy_out(f"ga.{B}", SG[:, B, 0:512])
            act.wait_ge(s_gd, 3)
            act.activation(gl, gd, ACT.Exp).then_inc(s_ge, 1)
            act.activation(gz, gd, ACT.Exp, scale=-1.0).then_inc(s_ge, 1)
            act.activation(ge, ge, ACT.Exp).then_inc(s_ge, 1)
            act.activation(sm(16, 8), gg.rearrange("p (q n i) -> p (q n) i", q=2, i=CHUNK)[:, :, CHUNK - 1],
                           ACT.Exp).then_inc(s_ge, 1)
            act.wait_ge(s_ge, 4)
            act.activation(gg, gg, ACT.Exp).then_inc(s_ge, 1)
            for name in ("qkb", "vb", "gb"):
                for B in range(NB):
                    dst = {"qkb": QKB[:, B, :], "vb": V[:, B, 512:1024], "gb": SG[:, B, 512:1024]}[name]
                    copy_out(f"{name}.{B}", dst)
            done(act, act.activation(SGf, SGf, ACT.Silu), s_silu)
            copy_out("rqT", QT[:, 2:4, :].rearrange("p q t -> p (q t)"))
            copy_out("rkT", KT[:, 2:4, :].rearrange("p q t -> p (q t)"))
            o = arrive(act, "kgT")
            took(act, act.activation(KI[:, :, 0:256], o[:, :].rearrange("p (b f) -> p b f", b=NB), ACT.Copy), "act")
            for B in range(NB):
                copy_out(f"sT.{B}", ST[:, B, :, :].rearrange("p h i -> p (h i)"))
            for i in range(4):
                copy_out(f"o.{i}", O[:, i // 2, 512 * (i % 2):512 * (i % 2) + 512])
            act.wait_ge(s_cen, 1)
            done(act, act.activation(SQ, Of, ACT.Square), s_sq)
            act.wait_ge(s_hvar, 1)
            done(act, act.activation(sm(40, 16), sm(24, 16), ACT.Sqrt), s_hrstd)
            for i in range(4):
                B, c0 = i // 2, 4 * (i % 2)
                o = arrive(act, f"oT.{i}")
                took(act, act.activation(MT[:, c0:c0 + 4, B * P:(B + 1) * P],
                                         o[:, :].rearrange("p (c t) -> p c t", c=4), ACT.Copy), "act")

            for layer in range(DEPTH):
                if layer:
                    act.wait_ge(s_const, 48)
                    done(act, act.activation(sm(100, 16), K("ldt"), ACT.Exp), s_par_a)
                    act.wait_ge(s_par_v, 2)
                    done(act, act.activation(sm(148, 16), sm(116, 16), ACT.Exp), s_par_a)
                    act.wait_ge(s_par_v, 3)
                    done(act, act.activation(sm(164, 16), sm(132, 16), ACT.Sin), s_par_a)
                    done(act, act.activation(sm(180, 16), sm(132, 16), ACT.Sin, scale=0.5), s_par_a)
                    norm_rstd(3)
                    for m in range(2):
                        copy_out(f"ucT.{m}", UC[:, 2 * m:2 * m + 2, :].rearrange("p c t -> p (c t)"))
                    for m in range(2):
                        copy_out(f"udT.{m}", UD[:, 2 * m:2 * m + 2, :].rearrange("p c t -> p (c t)"))
                    for m in range(2):
                        o = arrive(act, f"pmT.{m}")
                        step(act.activation(MT1[:, 2 * m, :], o[:, 0:256], ACT.Copy, scale=K("pscale", 2 * m, 1)))
                        took(act, act.activation(MT1[:, 2 * m + 1, :], o[:, 256:512], ACT.Copy,
                                                 scale=K("pscale", 2 * m + 1, 1)), "act")
                    for half in range(2):
                        act.wait_ge(s_ang, half + 1)
                        ang = YS[:, 0:2048]
                        act.activation(sinE.rearrange("p j t -> p (j t)"), ang, ACT.Sin).then_inc(s_sin, 1)
                        act.activation(cosE.rearrange("p j t -> p (j t)"), ang, ACT.Sin, scale=0.5).then_inc(s_sin, 1)
                    ready(act, "ys.1")
                    done(act, act.activation(Z.rearrange("p c t -> p (c t)"), YD.rearrange("p c t -> p (c t)"),
                                             ACT.Gelu), s_z)
                    for m in range(2):
                        o = arrive(act, f"glu.{m}")
                        for q in range(2):
                            ins = act.activation(P1[:, 2 * m + q, :], o[:, 256 * q:256 * q + 256], ACT.Sigmoid,
                                                 bias=K("bglu", 2 * m + q, 1))
                            if q:
                                took(act, ins, "act")
                            else:
                                step(ins)

                norm_rstd(1 + 3 * layer)
                ready(act, f"xnT{1 + 3 * layer}.3")
                if layer:
                    act.wait_ge(s_uused, 2 * NKEYS * layer)
                done(act, act.activation(xh, xnT[:, :, :], ACT.Copy), s_xh)
                for m in range(8):
                    copy_out(f"q{layer}.{m}", qT[:, 2 * m:2 * m + 2, :].rearrange("p g t -> p (g t)"))
                for i in range(8):
                    B, g0 = i // 4, 4 * (i % 4)
                    copy_out(f"scores{layer}.{i}", SC[:, B, g0:g0 + 4, :].rearrange("p g k -> p (g k)"))
                b0 = NKEYS * layer

                def high(b, h_, s, raws, loaded, parts, signal, used):
                    act.wait_ge(loaded[s], h_ * 16 + (8 * b0 + 16))
                    for half in range(2):
                        after(act, used, b * 2 + (2 * b0 + half - 1))
                        act.activation(parts[half], raws[s][:, 512 * half:512 * half + 512], ACT.Copy).then_inc(signal, 1)

                def high_u(b, h_, s):
                    high(b, h_, s, uraw, s_u, uh, s_uh, s_uused)

                def high_v(b, h_, s):
                    high(b, h_, s, vraw, s_v, vh, s_vh, s_vused)

                def gelu(b, s, dst):
                    act.wait_ge(s_uused, b * 2 + (2 * b0 + 2))
                    act.activation(dst, banks[s][:, 0:SEQ], ACT.Gelu).then_inc(s_gelu, 1)

                def ahead(b, h_, s):
                    high_u(b + 1, h_ + s, 1 - s)
                    gelu(b, s, big[:, bass.ds(b * SEQ, SEQ)])

                act.wait_ge(pe_out, NUMBER[f"q{layer}.7"] + 1)
                high_u(0, 0, 0)
                for b in range(2):
                    ahead(b, 0, b)
                over_b(act, ahead, 2, AHEAD - 1)
                gelu(AHEAD - 1, (AHEAD - 1) % 2, big[:, (AHEAD - 1) * SEQ:AHEAD * SEQ])
                act.wait_ge(s_best, NB * (layer + 1))
                done(act, act.activation(tk[4], tk[4], ACT.Exp), s_exp)
                for B in range(NB):
                    o = arrive(act, f"routes{layer}.{B}")
                    took(act, act.activation(routesT[:, :, B * P:(B + 1) * P],
                                             o[:, 0:384].rearrange("p (k t) -> p k t", k=3), ACT.Copy), "act")
                with act.Fori(0, NG // 4) as it:
                    for k in range(4):
                        act.wait_ge(s_wps, it * 4 + (NG * layer + k + 1))
                        act.activation(W[:, AHEAD:NKEYS, bass.ds(it * 16 + 4 * k, 4)],
                                       banks[k][:, :].rearrange("p (t b) -> p b t", t=4)[:, AHEAD:NKEYS, :],
                                       ACT.Copy).then_inc(s_wsb, 1)
                for b in range(2):
                    high_v(b, 0, b)
                over_b(act, high_v, 2, AHEAD - 1)
                high_u(AHEAD, AHEAD // 2, 0)
                high_v(AHEAD - 1, AHEAD // 2 - 1, 1)

                def gelu_v(b, h_, s):
                    gelu(b, s, banks[s][:, 0:SEQ])
                    high_v(b, h_, s)

                def u_gelu_v(b, h_, s):
                    high_u(b + 1, h_ + s, 1 - s)
                    gelu_v(b, h_, s)

                over_b(act, u_gelu_v, AHEAD, NKEYS - 1)
                gelu_v(NKEYS - 1, NKEYS // 2 - 1, 1)
                norm_rstd(2 + 3 * layer)
                for i in range(4):
                    copy_out(f"gate{layer}.{i}", GT[:, i // 2, 512 * (i % 2):512 * (i % 2) + 512], func=ACT.Sigmoid)
            norm_rstd(6)

        @block.gpsimd
        def _(pool):
            for B in range(NB):
                ready(pool, f"sT.{B}")
                for p in range(2):
                    v = ST[CHUNK * p:CHUNK * p + CHUNK, B, 0:4, :]
                    done(pool, pool.affine_select(out=v, in_=v, compare_op=ALU.is_ge, fill=0.0, base=0,
                                                  pattern=[[0, 4], [1, CHUNK]], channel_multiplier=-1), s_masked_p)
            for layer in range(DEPTH):

                def low_u(b, h_, s):
                    for half in range(2):
                        pool.wait_ge(s_uh, b * 2 + (2 * NKEYS * layer + half + 1))
                        pool.tensor_tensor(ul[half], uraw[s][:, 512 * half:512 * half + 512], uh[half].bitcast(F32),
                                           ALU.subtract).then_inc(s_ul, 1)

                over_b(pool, low_u, 0, AHEAD)

        @block.vector
        def _(dve):
            def step(ins):
                done(dve, ins, v_step)

            def bcast(ap, shape, axis):
                return ap.unsqueeze(axis).to_broadcast(shape)

            def norm_scale(site):
                for B in range(NB):
                    step(dve.tensor_tensor_reduce(xs[:, B, :], h[:, B, :], h[:, B, :], 1.0, 0.0, ALU.mult, ALU.add,
                                                  sm(B, 1)))
                step(dve.tensor_scalar(sm(0, 2), sm(0, 2), 1.0 / D, EPS, ALU.mult, ALU.add))
                done(dve, dve.reciprocal(sm(2, 2), sm(0, 2)), s_var)
                dve.wait_ge(s_rstd, site + 1)

            def norm(site):
                norm_scale(site)
                for B in range(NB):
                    done(dve, dve.tensor_scalar(xs[:, B, :], h[:, B, :], sm(4 + B, 1), None, ALU.mult), s_xs)
                for i in range(4):
                    B, c0 = i // 2, 4 * (i % 2)
                    o = arrive(dve, f"xnT{site}.{i}")
                    w = K(SITES[site], c0, 4)
                    took(dve, dve.tensor_tensor(xnT[:, c0:c0 + 4, B * P:(B + 1) * P],
                                                o[:, :].rearrange("p (c t) -> p c t", c=4),
                                                bcast(w, [P, 4, P], 2), ALU.mult), "dve")

            def add_to_h(name):
                for i in range(4):
                    o = arrive(dve, f"{name}.{i}")
                    hv = h[:, i // 2, 512 * (i % 2):512 * (i % 2) + 512]
                    took(dve, dve.tensor_tensor(hv, hv, o[:, :], ALU.add), "dve")

            def reduce_angle(ang, k):
                step(dve.tensor_scalar(k, ang, 1.0 / TWO_PI, ROUND, ALU.mult, ALU.add))
                step(dve.tensor_scalar(k, k, -ROUND, None, ALU.add))
                for c in (C1, C2, C3):
                    step(dve.scalar_tensor_tensor(out=ang, in0=k, scalar=-c, in1=ang, op0=ALU.mult, op1=ALU.add))
                return dve.tensor_scalar(ang, ang, PI_LOW, -PI_LOW, ALU.min, ALU.max)

            dve.wait_ge(s_x, 16)
            dve.wait_ge(s_const, 48)
            norm(0)
            step(dve.tensor_copy(sm(8, 2), posi[:, :]))
            for B in range(NB):
                step(dve.tensor_scalar(trig[0][:, 32 * B:32 * B + 32], C("freq"), sm(8 + B, 1), None, ALU.mult))
            done(dve, reduce_angle(trig[0], trig[1]), s_rope_ang)
            o = arrive(dve, "zT")
            z3 = gz.rearrange("p (q t) -> p q t", q=2)
            took(dve, dve.tensor_tensor(z3, o[:, :].rearrange("p (q t) -> p q t", q=2),
                                        bcast(K("bup"), [P, 2, SEQ], 2), ALU.add), "dve")
            done(dve, dve.scalar_tensor_tensor(out=ge, in0=gz, scalar=-1.0, in1=gz, op0=ALU.mult, op1=ALU.max), s_log)
            step(dve.tensor_scalar(gz, gz, 0.0, None, ALU.min))
            dve.wait_ge(s_rope_sin, 2)
            step(dve.tensor_tensor(trig[3], trig[3], trig[3], ALU.mult))
            step(dve.tensor_scalar(trig[3], trig[3], -2.0, 1.0, ALU.mult, ALU.add))
            dve.wait_ge(s_loga, 1)
            step(dve.tensor_tensor(gz, gz, gl, ALU.subtract))
            step(dve.tensor_scalar(gz, gz, 1.0 / GATE_NORM, None, ALU.mult))
            for q in range(2):
                step(dve.tensor_tensor_scan(gg[:, 256 * q:256 * q + 256], C("starts"), gz[:, 256 * q:256 * q + 256],
                                            0.0, ALU.mult, ALU.add))
            g3 = gg.rearrange("p (n i) -> p n i", i=CHUNK)
            last3 = g3[:, :, CHUNK - 1]
            step(dve.tensor_scalar(sm(56, 8), last3, 0.5, None, ALU.mult))
            done(dve, dve.tensor_tensor(gd.rearrange("p (n i) -> p n i", i=CHUNK), g3,
                                        bcast(sm(56, 8), [P, 8, CHUNK], 2), ALU.subtract), s_gd)
            step(dve.tensor_copy(sm(64, 8), last3))
            done(dve, dve.tensor_tensor(ge.rearrange("p (n i) -> p n i", i=CHUNK),
                                        bcast(sm(64, 8), [P, 8, CHUNK], 2), g3, ALU.subtract), s_gd)
            done(dve, dve.tensor_copy(sm(72, 2), C("gend")), s_gd)
            dve.wait_ge(s_ge, 5)
            ready(dve, "kaT")
            gate3 = [g.rearrange("p (q t) -> p q t", q=2) for g in (gl, gz, gg, ge)]
            done(dve, dve.tensor_tensor(QT[:, 0:2, :], qraw, gate3[0], ALU.mult), s_qt)
            done(dve, dve.tensor_tensor(KT[:, 0:2, :], kraw, gate3[1], ALU.mult), s_qt)
            done(dve, dve.tensor_tensor(QI[:, 0:2, :], qraw, gate3[2], ALU.mult), s_qt)
            done(dve, dve.tensor_tensor(kraw, kraw, gate3[3], ALU.mult), s_qt)
            sinr, cosr = trig[2], trig[3]
            tmp = SQf = STATE.rearrange("p n q e -> p (n q e)")
            for B in range(NB):
                ready(dve, f"qkb.{B}")
                xv = QKB[:, B, :].rearrange("p (h two r) -> p h two r", two=2, r=32)
                yv = ROT[:, B, :].rearrange("p (h two r) -> p h two r", two=2, r=32)
                cb_ = bcast(cosr[:, 32 * B:32 * B + 32], [P, 8, 32], 1)
                sb_ = bcast(sinr[:, 32 * B:32 * B + 32], [P, 8, 32], 1)
                t_ = [tmp[:, 256 * i:256 * i + 256].rearrange("p (h r) -> p h r", h=8) for i in range(4)]
                dve.tensor_tensor(t_[0], xv[:, :, 0, :], cb_, ALU.mult).then_inc(v_step, 1)
                dve.tensor_tensor(t_[1], xv[:, :, 1, :], sb_, ALU.mult).then_inc(v_step, 1)
                dve.tensor_tensor(t_[2], xv[:, :, 1, :], cb_, ALU.mult).then_inc(v_step, 1)
                count[v_step] += 3
                step(dve.tensor_tensor(t_[3], xv[:, :, 0, :], sb_, ALU.mult))
                step(dve.tensor_tensor(yv[:, :, 0, :], t_[0], t_[1], ALU.subtract))
                done(dve, dve.tensor_tensor(yv[:, :, 1, :], t_[2], t_[3], ALU.add), s_rot)
            for B in range(NB):
                done(dve, dve.tensor_tensor(KI[:, B, 256:512].rearrange("p (h d) -> p h d", h=4),
                                            ROT[:, B, 256:512].rearrange("p (h d) -> p h d", h=4),
                                            bcast(C("kdec"), [P, 4, HD], 2), ALU.mult), s_ret)
            ready(dve, "rqT")
            qd = C("qdec").rearrange("p (q i) -> p q i", q=2)
            for q in range(2):
                ins = dve.tensor_tensor(QI[:, 2 + q, :].rearrange("p (n i) -> p n i", i=CHUNK),
                                        QT[:, 2 + q, :].rearrange("p (n i) -> p n i", i=CHUNK),
                                        bcast(qd[:, q, :], [P, 4, CHUNK], 1), ALU.mult)
                if q:
                    done(dve, ins, s_ret)
                else:
                    step(ins)
            rm = C("retmask").rearrange("p (h i) -> p h i", h=4)
            for B in range(NB):
                ready(dve, f"sT.{B}")
                v = ST[:, B, 4:8, :]
                done(dve, dve.tensor_tensor(v, v, rm, ALU.mult), s_masked_v)
            for n in range(3):
                o = arrive(dve, f"kv.{n}")
                if n == 0:
                    took(dve, dve.tensor_copy(STATE[:, 0, :, :].rearrange("p q e -> p (q e)"), o[:, :]), "dve")
                else:
                    for q in range(PAIRS):
                        dec = sm(16 + 4 * q + n, 1) if q < 2 else sm(72 + q - 2, 1)
                        ins = dve.scalar_tensor_tensor(out=STATE[:, n, q, :], in0=STATE[:, n - 1, q, :], scalar=dec,
                                                       in1=o[:, P * q:P * q + P], op0=ALU.mult, op1=ALU.add)
                        if q == PAIRS - 1:
                            took(dve, ins, "dve")
                        else:
                            step(ins)
            ready(dve, "o.3")
            for B in range(NB):
                v = O[:, B, 512:1024].rearrange("p (h e) -> p h e", h=4)
                step(dve.tensor_reduce(sm(80, 4), v, AX_X, ALU.add))
                step(dve.tensor_scalar(sm(80, 4), sm(80, 4), 1.0 / P, None, ALU.mult))
                ins = dve.tensor_tensor(v, v, bcast(sm(80, 4), [P, 4, P], 2), ALU.subtract)
                if B:
                    done(dve, ins, s_cen)
                else:
                    step(ins)
            dve.wait_ge(s_sq, 1)
            step(dve.tensor_reduce(sm(24, 16), SQ.rearrange("p (g e) -> p g e", e=P), AX_X, ALU.add))
            step(dve.tensor_scalar(sm(24, 16), sm(24, 16), 1.0 / P, EPS, ALU.mult, ALU.add))
            done(dve, dve.reciprocal(sm(24, 16), sm(24, 16)), s_hvar)
            dve.wait_ge(s_hrstd, 1)
            dve.wait_ge(s_row, 16)
            dve.wait_ge(s_silu, 1)
            o16 = Of.rearrange("p (g e) -> p g e", e=P)
            step(dve.tensor_tensor(o16, o16, bcast(sm(40, 16), [P, 16, P], 2), ALU.mult))
            step(dve.tensor_tensor(O, O, bcast(mix_row, [P, NB, D], 1), ALU.mult))
            done(dve, dve.tensor_tensor(Of, Of, SGf, ALU.mult), s_oready)
            add_to_h("mix0")

            for layer in range(DEPTH):
                if layer:
                    dve.wait_ge(s_par_a, 1)
                    done(dve, dve.tensor_tensor(sm(116, 16), K("are"), sm(100, 16), ALU.mult), s_par_v)
                    done(dve, dve.tensor_tensor(sm(132, 16), K("aim"), sm(100, 16), ALU.mult), s_par_v)
                    done(dve, reduce_angle(sm(132, 16), sm(196, 16)), s_par_v)
                    dve.wait_ge(s_par_a, 4)
                    step(dve.tensor_tensor(sm(180, 16), sm(180, 16), sm(180, 16), ALU.mult))
                    step(dve.tensor_scalar(sm(180, 16), sm(180, 16), -2.0, 1.0, ALU.mult, ALU.add))
                    step(dve.tensor_tensor(sm(212, 16), sm(148, 16), sm(180, 16), ALU.mult))
                    step(dve.tensor_scalar(sm(212, 16), sm(212, 16), -1.0, None, ALU.add))
                    step(dve.tensor_tensor(sm(228, 16), sm(148, 16), sm(164, 16), ALU.mult))
                    step(dve.tensor_tensor(sm(244, 16), K("are"), K("are"), ALU.mult))
                    step(dve.tensor_tensor(sm(260, 16), K("aim"), K("aim"), ALU.mult))
                    step(dve.tensor_tensor(sm(244, 16), sm(244, 16), sm(260, 16), ALU.add))
                    step(dve.reciprocal(sm(244, 16), sm(244, 16)))
                    step(dve.tensor_tensor(sm(276, 16), sm(212, 16), K("are"), ALU.mult))
                    step(dve.tensor_tensor(sm(260, 16), sm(228, 16), K("aim"), ALU.mult))
                    step(dve.tensor_tensor(sm(276, 16), sm(276, 16), sm(260, 16), ALU.add))
                    step(dve.tensor_tensor(sm(276, 16), sm(276, 16), sm(244, 16), ALU.mult))
                    step(dve.tensor_tensor(sm(292, 16), sm(228, 16), K("are"), ALU.mult))
                    step(dve.tensor_tensor(sm(260, 16), sm(212, 16), K("aim"), ALU.mult))
                    step(dve.tensor_tensor(sm(292, 16), sm(292, 16), sm(260, 16), ALU.subtract))
                    step(dve.tensor_tensor(sm(292, 16), sm(292, 16), sm(244, 16), ALU.mult))
                    norm(3)
                    dve.wait_ge(s_s5, 32)
                    cre = bcast(sm(276, 16), [P, S5_TILES, 32], 2)
                    cim = bcast(sm(292, 16), [P, S5_TILES, 32], 2)
                    ta = WS[:, 0:512].rearrange("p (j n) -> p j n", n=32)
                    step(dve.tensor_tensor(ta, s5c[:, 1, :, :], cim, ALU.mult))
                    step(dve.tensor_tensor(s5d[:, 0, :, :], s5c[:, 0, :, :], cre, ALU.mult))
                    step(dve.tensor_tensor(s5d[:, 0, :, :], s5d[:, 0, :, :], ta, ALU.subtract))
                    step(dve.tensor_tensor(ta, s5c[:, 0, :, :], cim, ALU.mult))
                    step(dve.tensor_tensor(s5d[:, 1, :, :], s5c[:, 1, :, :], cre, ALU.mult))
                    step(dve.tensor_tensor(s5d[:, 1, :, :], s5d[:, 1, :, :], ta, ALU.add))
                    done(dve, dve.tensor_scalar(s5d[:, 1, :, :], s5d[:, 1, :, :], -1.0, None, ALU.mult), s_c)

                    def angles(half):
                        a3 = YS[:, 0:2048].rearrange("p (j t) -> p j t", j=8)
                        step(dve.tensor_tensor(a3, bcast(C("time"), [P, 8, SEQ], 1),
                                               bcast(sm(132 + 8 * half, 8), [P, 8, SEQ], 2), ALU.mult))
                        done(dve, reduce_angle(YS[:, 0:2048], YS[:, 2048:4096]), s_ang)

                    angles(0)
                    ready(dve, "ucT.1")
                    dve.wait_ge(s_late, 48)
                    src, dst = UC, P1
                    for k, w in enumerate((1, 2, 4, 8)):
                        step(dve.tensor_copy(dst[:, k:4, 0:w], src[:, k:4, 0:w]))
                        step(dve.tensor_tensor(dst[:, k:4, w:SEQ], src[:, k:4, w:SEQ], src[:, k:4, 0:SEQ - w], ALU.add))
                        src, dst = dst, (P2 if dst is P1 else P1)
                    for g in range(4):
                        s_ = P1 if g % 2 == 0 else P2
                        step(dve.tensor_tensor(PM[:, g, :], s_[:, g, :], INV[:, g, :], ALU.mult))
                    done(dve, dve.tensor_tensor(PM, PM, UC, ALU.subtract), s_pool)
                    v4 = VS.rearrange("p (r j t) -> p r j t", r=2, j=8)
                    y4 = YS.rearrange("p (r j t) -> p r j t", r=2, j=8)
                    w4 = WS.rearrange("p (r j t) -> p r j t", r=2, j=8)
                    for half in range(2):
                        if half:
                            angles(1)
                        dve.wait_ge(s_sin, 2 * half + 2)
                        c2 = cosE.rearrange("p j t -> p (j t)")
                        step(dve.tensor_tensor(c2, c2, c2, ALU.mult))
                        step(dve.tensor_scalar(c2, c2, -2.0, 1.0, ALU.mult, ALU.add))
                        m1 = WS[:, 0:512].rearrange("p (r t) -> p r t", r=2)
                        m2 = WS[:, 512:1024].rearrange("p (r t) -> p r t", r=2)
                        for j in range(8):
                            o = arrive(dve, f"bu.{8 * half + j}")
                            b3 = o[:, :].rearrange("p (r t) -> p r t", r=2)
                            step(dve.tensor_tensor(m1, b3, bcast(cosE[:, j, :], [P, 2, SEQ], 1), ALU.mult))
                            took(dve, dve.tensor_tensor(m2, b3, bcast(sinE[:, j, :], [P, 2, SEQ], 1), ALU.mult), "dve")
                            step(dve.tensor_tensor(v4[:, 0, j, :], m1[:, 0, :], m2[:, 1, :], ALU.add))
                            step(dve.tensor_tensor(v4[:, 1, j, :], m1[:, 1, :], m2[:, 0, :], ALU.subtract))
                            mag = sm(148 + 8 * half + j, 1).to_broadcast([P, SEQ])
                            for ri in range(2):
                                ins = dve.tensor_tensor_scan(y4[:, ri, j, :], mag, v4[:, ri, j, :], 0.0, ALU.mult, ALU.add)
                                step(ins)
                        for ri in range(2):
                            step(dve.tensor_tensor(v4[:, ri, :, :], y4[:, ri, :, :], cosE, ALU.mult))
                            step(dve.tensor_tensor(w4[:, ri, :, :], y4[:, ri, :, :], sinE, ALU.mult))
                        step(dve.tensor_tensor(v4[:, 0, :, :], v4[:, 0, :, :], w4[:, 1, :, :], ALU.subtract))
                        done(dve, dve.tensor_tensor(v4[:, 1, :, :], v4[:, 1, :, :], w4[:, 0, :, :], ALU.add), s_xst)
                        o = arrive(dve, f"ys.{half}")
                        for q in range(2):
                            f = 2 * half + q
                            ins = dve.scalar_tensor_tensor(out=YD[:, f, :], in0=UD[:, f, :], scalar=K("dskip", f, 1),
                                                           in1=o[:, 256 * q:256 * q + 256], op0=ALU.mult, op1=ALU.add)
                            if q:
                                took(dve, ins, "dve")
                            else:
                                step(ins)
                    dve.wait_ge(s_z, 1)
                    ready(dve, "glu.1")
                    done(dve, dve.tensor_tensor(MT1[:, 4:8, :], Z, P1, ALU.mult), s_mt)
                    add_to_h("mix1")

                norm(1 + 3 * layer)
                dve.wait_ge(s_xh, layer + 1)
                done(dve, dve.tensor_tensor(xl, xnT[:, :, :], xh.bitcast(F32), ALU.subtract), s_xl)
                idx = tk[0].bitcast(U32).rearrange("p (g k) -> p g k", g=HP)
                top = tk[1].rearrange("p (g k) -> p g k", g=HP)
                idf = tk[2].rearrange("p (g k) -> p g k", g=HP)
                for B in range(NB):
                    def top16(vals, index, data, n):
                        for r in range(2):
                            for i in range(n):
                                dve.max(out=vals(i)[:, 8 * r:8 * r + 8], in_=data(i)).then_inc(v_step, 1)
                            count[v_step] += n
                            dve.wait_ge(v_step, count[v_step])
                            for i in range(n):
                                dve.max_index(index(i)[:, 8 * r:8 * r + 8], vals(i)[:, 8 * r:8 * r + 8],
                                              data(i)).then_inc(v_step, 1)
                            count[v_step] += n
                            dve.wait_ge(v_step, count[v_step])
                            if r == 0:
                                for i in range(n):
                                    dve.match_replace(data(i), vals(i)[:, 0:8], data(i), LOWEST).then_inc(v_step, 1)
                                count[v_step] += n
                                dve.wait_ge(v_step, count[v_step])

                    ready(dve, f"scores{layer}.{4 * B + 3}")
                    top16(lambda i: top[:, i, :], lambda i: idx[:, i, :], lambda i: SC[:, B, i, :], HP)
                    step(dve.tensor_copy(tk[2], tk[0].bitcast(U32)))
                    c4 = CAND.rearrange("p h (i j) -> p h i j", i=TOPK)
                    t4 = top.rearrange("p (h two) k -> p h two k", two=2)
                    step(dve.tensor_tensor(c4, bcast(t4[:, :, 0, :], [P, PH, TOPK, TOPK], 3),
                                           bcast(t4[:, :, 1, :], [P, PH, TOPK, TOPK], 2), ALU.add))
                    best = tk[4][:, P * B:P * B + P].rearrange("p (h k) -> p h k", h=PH)
                    flat = tk[3][:, 0:P].bitcast(U32).rearrange("p (h k) -> p h k", h=PH)
                    top16(lambda i: best[:, i, :], lambda i: flat[:, i, :], lambda i: CAND[:, i, :], PH)
                    step(dve.tensor_copy(sm(320, 8), best[:, :, 0]))
                    done(dve, dve.tensor_tensor(best, best, bcast(sm(320, 8), [P, PH, TOPK], 2), ALU.subtract), s_best)
                    fu = tk[3][:, 0:P].bitcast(U32)
                    hi_lo = tk[3][:, P:2 * P].bitcast(U32)
                    id4 = idf.rearrange("p (h two) k -> p h two k", two=2)
                    for side in range(2):
                        if side == 0:
                            step(dve.tensor_scalar(hi_lo, fu, 4, None, ALU.logical_shift_right))
                        else:
                            step(dve.tensor_scalar(hi_lo, fu, TOPK - 1, None, ALU.bitwise_and))
                        which = sm(330, P)
                        step(dve.tensor_copy(which, hi_lo))
                        e4 = EQ.rearrange("p (h k i) -> p h k i", h=PH, k=TOPK)
                        e3 = EQ.rearrange("p (g i) -> p g i", i=TOPK)
                        step(dve.tensor_tensor(e3, bcast(which, [P, P, TOPK], 2), bcast(C("iota16"), [P, P, TOPK], 1),
                                               ALU.is_equal))
                        step(dve.tensor_tensor(e4, e4, bcast(id4[:, :, side, :], [P, PH, TOPK, TOPK], 2), ALU.mult))
                        step(dve.tensor_reduce(tk[5 + side][:, P * B:P * B + P], e3, AX_X, ALU.add))
                dve.wait_ge(s_exp, layer + 1)
                for B in range(NB):
                    best = tk[4][:, P * B:P * B + P].rearrange("p (h k) -> p h k", h=PH)
                    step(dve.tensor_reduce(sm(320, 8), best, AX_X, ALU.add))
                    step(dve.reciprocal(sm(320, 8), sm(320, 8)))
                    done(dve, dve.tensor_tensor(tk[7][:, P * B:P * B + P].rearrange("p (h k) -> p h k", h=PH), best,
                                                bcast(sm(320, 8), [P, PH, TOPK], 2), ALU.mult), s_route)
                ready(dve, f"routes{layer}.1")
                iota = C("iota")

                def onehots(g, k, first):
                    if not first:
                        dve.wait_ge(s_wps, g + (NG * layer - 1))
                    for t in range(4):
                        dve.tensor_scalar(OH[:, k % 2, 0, t, :], iota, routesT[:, 0, bass.ds(g * 4 + t, 1)],
                                          routesT[:, 2, bass.ds(g * 4 + t, 1)], ALU.is_equal, ALU.mult)
                    dve.tensor_tensor(OH[:, k % 2, 1, :, :], bcast(iota, [P, 4, NKEYS], 1),
                                      bcast(routesT[:, 1, bass.ds(g * 4, 4)], [P, 4, NKEYS], 2),
                                      ALU.is_equal).then_inc(s_ab, 1)

                def times_hidden(g, k):
                    dve.wait_ge(s_wsb, g + (NG * layer + 1))
                    wv = W[:, 0:AHEAD, bass.ds(g * 4, 4)]
                    dve.tensor_tensor(wv, banks[k][:, :].rearrange("p (t b) -> p b t", t=4)[:, 0:AHEAD, :], wv,
                                      ALU.mult).then_inc(s_wmul, 1)

                for g in range(4):
                    onehots(g, g, g < 2)
                    if g >= 2:
                        times_hidden(g - 2, g - 2)
                with dve.Fori(1, NG // 4) as it:
                    for k in range(4):
                        onehots(it * 4 + k, k, False)
                        times_hidden(it * 4 + (k - 2), (k - 2) % 4)
                for g in range(NG - 2, NG):
                    times_hidden(g, g % 4)
                b0 = NKEYS * layer
                dve.wait_ge(s_wmul, NG * (layer + 1))

                def low(b, s, raws, hi, lo, from_act, signal):
                    for half in range(2):
                        dve.wait_ge(from_act, b * 2 + (2 * b0 + half + 1))
                        dve.tensor_tensor(lo[half], raws[s][:, 512 * half:512 * half + 512], hi[half].bitcast(F32),
                                          ALU.subtract).then_inc(signal, 1)

                def two_parts(b, s, src):
                    dve.tensor_copy(ph[s], src).then_inc(s_pf, 1)
                    dve.wait_ge(s_pf, b + (b0 + 1))
                    dve.tensor_tensor(pl[s], src, ph[s].bitcast(F32), ALU.subtract).then_inc(s_p, 1)

                def stored(b, h_, s):
                    after(dve, s_vused, b * 2 + (2 * b0 - 2))
                    two_parts(b, s, W[:, bass.ds(b, 1), :].rearrange("p o t -> p (o t)"))
                    low(b, s, vraw, vh, vl, s_vh, s_vl)

                def gate_and_v(b, h_, s):
                    dve.wait_ge(s_gelu, b + (b0 + 1))
                    dve.wait_ge(s_vused, b * 2 + (2 * b0 - 2))
                    dve.tensor_tensor(PF[s], banks[s][:, 0:SEQ], W[:, bass.ds(b, 1), :].rearrange("p o t -> p (o t)"),
                                      ALU.mult).then_inc(s_pm, 1)
                    dve.wait_ge(s_pm, b + ((NKEYS - AHEAD) * layer - AHEAD + 1))
                    two_parts(b, s, PF[s])
                    low(b, s, vraw, vh, vl, s_vh, s_vl)

                def u_gate_v(b, h_, s):
                    low(b + 1, 1 - s, uraw, uh, ul, s_uh, s_ul)
                    gate_and_v(b, h_, s)

                for b in range(2):
                    stored(b, 0, b)
                over_b(dve, stored, 2, AHEAD - 1)
                low(AHEAD, 0, uraw, uh, ul, s_uh, s_ul)
                stored(AHEAD - 1, None, 1)
                over_b(dve, u_gate_v, AHEAD, NKEYS - 1)
                gate_and_v(NKEYS - 1, None, 1)
                dve.wait_ge(s_vused, 2 * NKEYS * (layer + 1))
                for i in range(4):
                    hv = h[:, i // 2, 512 * (i % 2):512 * (i % 2) + 512]
                    step(dve.tensor_tensor(hv, hv, banks[4 + i][:, :], ALU.add))
                norm(2 + 3 * layer)
                for i in range(4):
                    ready(dve, f"gate{layer}.{i}")
                    gv = GT[:, i // 2, 512 * (i % 2):512 * (i % 2) + 512]
                    hv = h[:, i // 2, 512 * (i % 2):512 * (i % 2) + 512]
                    o = arrive(dve, f"ple{layer}.{i}")
                    step(dve.tensor_tensor(gv, gv, o[:, :], ALU.mult))
                    took(dve, dve.tensor_tensor(hv, hv, gv, ALU.add), "dve")
            norm_scale(6)
            dve.wait_ge(s_row, 32)
            for B in range(NB):
                done(dve, dve.scalar_tensor_tensor(out=xs[:, B, :], in0=h[:, B, :], scalar=sm(4 + B, 1),
                                                   in1=final_row, op0=ALU.mult, op1=ALU.mult), s_fin)


def kernel(x, p, positions, norm_mix_w, norm_ffn_w, norm_ple_w, final_norm_w,
           ev_w_in, ev_gla_w_up, ev_gla_b_up, ev_gla_norm_w, ev_ret_norm_w, ev_w_out,
           od_w_in, od_pool_w, od_pool_scale, od_s5_a_re, od_s5_a_im, od_s5_log_dt,
           od_s5_b_re, od_s5_b_im, od_s5_c_re, od_s5_c_im, od_s5_d, od_s5_w_glu, od_s5_b_glu, od_w_out,
           peer_w_q, peer_sub_keys, peer_u, peer_v, ple_w_proj, ple_w_gate):
    import concourse.bacc as bacc
    from concourse.bass_utils import run_bass_kernel_spmd

    def arr(a):
        return np.asarray(a)

    def tiles(a):
        a = arr(a)
        return a.reshape(-1, P, a.shape[-1]).transpose(1, 0, 2)

    def column(a):
        return arr(a).reshape(-1, P).T

    w_in = arr(ev_w_in)[0]
    q_a, k_a, v_a, g_a, r_a, q_b, k_b, v_b, g_b = np.split(
        w_in, np.cumsum([256, 256, 512, 512, GATE_RANK, 256, 256, 512])[:8], axis=1)
    groups = [np.concatenate([q_a, k_a], 1), v_a, g_a, np.concatenate([q_b, k_b], 1), v_b, g_b]
    consts, counts = constants()
    cols = np.concatenate(
        [column(a) for l in range(DEPTH) for a in (arr(norm_mix_w)[l], arr(norm_ffn_w)[l], arr(norm_ple_w)[l])]
        + [column(ev_gla_b_up), column(od_pool_scale), column(od_s5_d), column(od_s5_b_glu), column(od_s5_a_re),
           column(od_s5_a_im), column(np.repeat(arr(od_s5_log_dt).reshape(-1), HD))], axis=1)
    rows = np.concatenate([np.tile(arr(ev_gla_norm_w)[0], 4), arr(ev_ret_norm_w)[0], arr(final_norm_w)])
    s5_b = np.zeros((4, 2, 16, 4, 2, 2, HD), np.float32)
    s5_c = np.zeros((2, HD, 2, S5_TILES, 2, 16), np.float32)
    for r, (b, c) in enumerate(((od_s5_b_re, od_s5_c_re), (od_s5_b_im, od_s5_c_im))):
        b = arr(b)[0].reshape(4, 4, 2, HD, 16)
        c = arr(c)[0].reshape(S5_TILES, 2, 16, HD)
        for g in range(2):
            s5_b[:, g, :, :, r, g, :] = b[:, :, g].transpose(1, 3, 0, 2)
            s5_c[g, :, r, :, g, :] = c[:, g].transpose(2, 0, 1)
    data = {
        "consts": consts, "counts": counts.reshape(P, 4, SEQ), "cols": cols, "rows": np.tile(rows, (P, 1)),
        "pos": arr(positions).reshape(NB, P).T,
        "x": arr(x)[0].reshape(NB, P, D).transpose(1, 0, 2),
        "pT": arr(p)[:, 0].transpose(0, 2, 1).reshape(DEPTH, 2, P, SEQ).transpose(0, 2, 1, 3),
        "w_even": np.stack([tiles(g) for g in groups]), "w_ra": tiles(r_a), "w_up": arr(ev_gla_w_up)[0],
        "w_out0": tiles(arr(ev_w_out)[0]), "w_odd": tiles(arr(od_w_in)[0]),
        "w_pool": arr(od_pool_w)[0].transpose(1, 0, 2),
        "s5_b": s5_b.reshape(P, 4, 2, P), "s5_c": s5_c.reshape(P, 2, S5_TILES, 32),
        "w_glu": tiles(arr(od_s5_w_glu)[0]), "w_out1": tiles(arr(od_w_out)[0]),
        "w_q": np.stack([tiles(w) for w in arr(peer_w_q)]),
        "keys": arr(peer_sub_keys).reshape(DEPTH, HP, NKEYS, P).transpose(0, 3, 1, 2),
        "u_tab": arr(peer_u).reshape(DEPTH, NKEYS, NKEYS, DC, P).transpose(0, 2, 4, 3, 1).reshape(DEPTH, NKEYS, P, D),
        "v_tab": arr(peer_v).reshape(DEPTH, NKEYS, NKEYS, D).transpose(0, 2, 1, 3),
        "w_ple": np.stack([tiles(w) for w in arr(ple_w_proj)]),
        "w_gate": np.stack([tiles(w) for w in arr(ple_w_gate)]),
    }
    data = {f"in_{n}": np.ascontiguousarray(a) for n, a in data.items()}
    nc = bacc.Bacc("TRN2", target_bir_lowering=False, num_devices=1)
    args = {n[3:]: nc.dram_tensor(n, a.shape, mybir.dt.from_np(a.dtype), kind="ExternalInput").ap()
            for n, a in data.items()}
    out = nc.dram_tensor("out", (1, SEQ, D), F32, kind="ExternalOutput").ap()
    program(nc, out=out.rearrange("o (b p) d -> p (o b) d", p=P), **args)
    result = run_bass_kernel_spmd(nc, [data], core_ids=[0])
    return result.results[0]["out"]
```

```python
from contextlib import ExitStack

import numpy as np

import concourse.bass as bass
from concourse import mybir

ALU = mybir.AluOpType
ACT = mybir.ActivationFunctionType
F32 = mybir.dt.float32
F32R = mybir.dt.float32r
I32 = mybir.dt.int32
U32 = mybir.dt.uint32
AX_X = mybir.AxisListType.X

P = 128
SEQ = 256
NB = SEQ // P
D = 1024
DC = D // P
DEPTH = 2
EPS = 1e-6
CHUNK = 64
HEADS = 8
HD = 64
PAIRS = HEADS // 2
GATE_RANK = 16
GATE_NORM = 16.0
NKEYS = 128
TOPK = 16
PH = 8
HP = 2 * PH
S5_TILES = 16
AHEAD = 40
NG = SEQ // 4
PLE_FROM = 48
ODD_FROM = 98
WINDOWS = (2, 4, 8, 16)
TWO_PI = 2.0 * np.pi
ROUND = 1.5 * 2.0 ** 23
C1 = 6.28125
C2 = float(np.float32(TWO_PI - C1))
C3 = float(np.float32(TWO_PI - C1 - C2))
PI_LOW = 3.1415925
LOWEST = -3.4e38

OUTPUTS = []


def plan_outputs():
    def add(taker, *names):
        OUTPUTS.extend((n, taker) for n in names)

    def transposed(site):
        add("dve", *[f"xnT{site}.{i}" for i in range(4)])

    def peer(layer):
        add("act", *[f"q{layer}.{i}" for i in range(8)])
        add("act", *[f"scores{layer}.{i}" for i in range(8)])
        add("act", *[f"routes{layer}.{i}" for i in range(2)])

    def ple(layer):
        assert len(OUTPUTS) % 8 == 4
        add("act", *[f"ple{layer}.{i}" for i in range(4)])
        transposed(2 + 3 * layer)
        add("act", *[f"gate{layer}.{i}" for i in range(4)])

    OUTPUTS.clear()
    transposed(0)
    add("act", "qaT", "kaT", "raT")
    add("dve", "zT")
    for name in ("va", "ga", "qkb", "vb", "gb"):
        add("act", *[f"{name}.{B}" for B in range(NB)])
    add("act", "rqT", "rkT", "kgT", "sT.0", "sT.1")
    add("dve", "kv.0", "kv.1", "kv.2")
    add("act", *[f"o.{i}" for i in range(4)])
    add("act", *[f"oT.{i}" for i in range(4)])
    add("dve", *[f"mix0.{i}" for i in range(4)])
    transposed(1)
    peer(0)
    ple(0)
    transposed(3)
    add("act", "udT.0", "udT.1")
    for half in range(2):
        add("dve", *[f"bu.{8 * half + j}" for j in range(8)])
        if half == 0:
            add("act", "ucT.0", "ucT.1")
        else:
            add("act", "pmT.0", "pmT.1")
            add("dve", *[f"mixp.{i}" for i in range(4)])
        add("dve", f"ys.{half}")
    add("act", "glu.0", "glu.1")
    add("dve", *[f"mix1.{i}" for i in range(4)])
    transposed(4)
    peer(1)
    ple(1)


plan_outputs()
NUMBER = {name: n for n, (name, _) in enumerate(OUTPUTS)}
RANK = {name: sum(t == taker for _, t in OUTPUTS[:n]) for n, (name, taker) in enumerate(OUTPUTS)}

CONST = {}


def constants():
    p = np.arange(P)
    lg = np.log(1.0 - 2.0 ** (-5.0 - np.arange(4)))
    j = p % CHUNK
    i = np.arange(CHUNK)
    scale = HD ** -0.5
    diff = i[None, None, :] - j[:, None, None]
    retmask = np.where(diff >= 0, np.exp(lg[None, :, None] * np.maximum(diff, 0)), 0.0) * scale
    head = 2 * np.arange(2)[None, :] + (p // HD)[:, None]
    qdec = np.exp(lg[head][:, :, None] * (i + 1.0))
    kdec = np.exp(lg[None, :] * (CHUNK - 1.0 - j[:, None])) * scale
    gend = np.exp(lg[head] * CHUNK)
    freq = np.float32(10000.0) ** (-np.arange(32, dtype=np.float32) / np.float32(32))
    starts = (np.arange(SEQ) % CHUNK != 0).astype(np.float32)
    t = np.arange(SEQ)
    parts = [
        ("ident", np.eye(P)), ("iota", np.tile(p, (P, 1))), ("iota16", np.tile(p[:16], (P, 1))),
        ("gend", gend), ("kdec", kdec), ("freq", np.tile(freq, (P, 1))),
        ("retmask", retmask.reshape(P, -1)), ("qdec", qdec.reshape(P, -1)), ("starts", np.tile(starts, (P, 1))),
        ("time", np.tile(t, (P, 1))),
    ]
    at = 0
    for name, a in parts:
        CONST[name] = (at, at + a.shape[1])
        at += a.shape[1]
    count = np.stack([1.0 / np.minimum(t + 1.0, w) for w in WINDOWS])
    return (np.concatenate([a for _, a in parts], axis=1).astype(np.float32),
            np.tile(count.reshape(1, -1), (P, 1)).astype(np.float32))


NCONST = constants()[0].shape[1]

COL = {}
for _name, _w in (("mix0", 8), ("ffn0", 8), ("ple0", 8), ("mix1", 8), ("ffn1", 8), ("ple1", 8), ("bup", 2),
                  ("pscale", 4), ("dskip", 4), ("bglu", 4), ("are", 16), ("aim", 16), ("ldt", 16)):
    _at = sum(w for _, w in COL.values())
    COL[_name] = (_at, _w)
NCOL = sum(w for _, w in COL.values())
SPLIT = (1, 2, 4, 5)
SITES = ("mix0", "ffn0", "ple0", "mix1", "ffn1", "ple1")


def program(nc, consts, counts, cols, rows, pos, x, pT, w_even, w_ra, w_up, w_out0, w_odd, w_pool, s5_b, s5_c,
            w_glu, w_out1, w_q, keys, u_tab, v_tab, w_ple, out):
    with ExitStack() as ctx:
        def sb(name, shape, dt=F32):
            return ctx.enter_context(nc.sbuf_tensor(name, shape, dt))

        def sem(name):
            return ctx.enter_context(nc.semaphore(name))

        banks = [ctx.enter_context(nc.psum_tensor(f"bank{i}", [P, 512], F32)) for i in range(8)]
        sums, work = banks[0:4], banks[4:8]

        big = sb("big", [P, 32768])
        raw = sb("raw", [P, 4096])
        halves = sb("halves", [P, 9216], F32R)
        h = sb("h", [P, NB, D])
        xnT = sb("xnT", [P, DC, SEQ])
        cst = sb("cst", [P, NCONST])
        col = sb("col", [P, NCOL])
        posi = sb("posi", [P, NB], I32)
        routesT = sb("routesT", [P, 3, SEQ])
        small = sb("small", [P, 600])

        def C(name):
            a, b = CONST[name]
            return cst[:, a:b]

        def K(name, i=0, n=None):
            a, w = COL[name]
            return col[:, a + i:a + (i + n if n else w)]

        def region(base, a, n):
            return base[:, a:a + n]

        ident = C("ident")
        xs = region(big, 28672, 2048).rearrange("p (b f) -> p b f", b=NB)
        final_row = region(big, 20480, D)

        s_const = sem("const_loaded")
        s_x = sem("x_loaded")
        s_row = sem("rows_loaded")
        s_up = sem("wup_loaded")
        s_win = [sem(f"w_even_loaded{i}") for i in range(3)]
        s_wra = sem("w_ra_loaded")
        s_wout = sem("w_out_loaded")
        s_wq = [sem(f"w_q_loaded{i}") for i in range(4)]
        s_keys = sem("keys_loaded")
        s_ple = sem("ple_loaded")
        s_odd = sem("w_odd_loaded")
        s_s5 = sem("s5_loaded")
        s_counts = sem("window_counts_loaded")
        s_late = sem("glu_pool_loaded")
        s_raw = [sem(f"table_slot_loaded{i}") for i in range(4)]
        s_out = sem("out_stored")

        pe_out = sem("pe_output")
        taken = {"act": sem("act_took"), "dve": sem("dve_took")}
        v_step = sem("dve_step")
        a_step = sem("act_step")
        s_rows = sem("other_rows_done")
        s_var = sem("norm_var")
        s_rstd = sem("norm_rstd")
        s_added = sem("experts_added")
        s_emb = sem("embedding_added")
        s_square = sem("second_block_squared")
        s_xs = [sem(f"xs_ready{B}") for B in range(NB)]
        s_log = sem("gate_abs_ready")
        s_loga = sem("gate_log_ready")
        s_gd = sem("gate_sums_ready")
        s_ge = sem("gate_exp_ready")
        s_qt = sem("gla_qk_ready")
        s_rope_ang = sem("rope_angle_ready")
        s_rope_sin = sem("rope_sin_ready")
        s_rot = sem("rope_ready")
        s_ret = sem("ret_q_inter_ready")
        s_masked_v = sem("ret_scores_decayed")
        s_masked_p = sem("gla_scores_masked")
        s_cen = sem("heads_centred")
        s_sq = sem("heads_squared")
        s_hvar = sem("heads_var")
        s_hrstd = sem("heads_rstd")
        s_silu = sem("silu_ready")
        s_oready = sem("heads_out_ready")
        s_best = sem("best_minus_max")
        s_exp = sem("best_exp")
        s_route = sem("routes_ready")
        s_first = sem("first_onehots_ready")
        s_second = sem("second_onehots_ready")
        s_far = sem("second_distances_ready")
        s_near = sem("second_distances_absolute")
        s_wps = sem("w_psum_ready")
        s_wsb = sem("w_ready")
        s_wmul = sem("w_times_hidden")
        s_qh = sem("w_q_high_ready")
        s_ql = sem("w_q_low_ready")
        s_qused = sem("w_q_halves_used")
        s_gh = sem("w_gate_high_ready")
        s_gl = sem("w_gate_low_ready")
        s_gused = sem("w_gate_halves_used")
        s_xh = sem("x_high_ready")
        s_xl = sem("x_low_ready")
        s_uh = sem("u_high_ready")
        s_ul = sem("u_low_ready")
        s_uused = sem("u_halves_used")
        s_vh = sem("v_high_ready")
        s_vl = sem("v_low_ready")
        s_vused = sem("v_halves_used")
        s_gelu = sem("gelu_ready")
        s_pm = sem("gated_product")
        s_pf = sem("gated_high_ready")
        s_p = sem("gated_ready")
        s_par_a = sem("s5_par_act")
        s_par_v = sem("s5_par_dve")
        s_coef = sem("s5_coefficients_ready")
        p_step = sem("pool_step")
        s_ang = sem("s5_angles_ready")
        s_sin = sem("s5_sin_ready")
        s_c = sem("s5_c_ready")
        s_pool = sem("pooled_ready")
        s_xst = sem("s5_states_ready")
        s_turned = sem("s5_products_ready")
        s_drive = sem("s5_inputs_ready")
        s_z = sem("s5_z_ready")
        s_mt = sem("s5_out_ready")
        s_fin = sem("final_ready")

        count = {}

        def done(eng, ins, s):
            count[s] = count.get(s, 0) + 1
            ins.then_inc(s, 1)
            eng.wait_ge(s, count[s])

        def took(eng, ins, who):
            done(eng, ins, taken[who])

        def output(pe, name):
            n = NUMBER[name]
            if n >= 8:
                before, taker = OUTPUTS[n - 8]
                pe.wait_ge(taken[taker], RANK[before] + 1)
            return banks[n % 8]

        def arrive(eng, name):
            eng.wait_ge(pe_out, NUMBER[name] + 1)
            return banks[NUMBER[name] % 8]

        def ready(eng, name):
            eng.wait_ge(taken[dict(OUTPUTS)[name]], RANK[name] + 1)

        wring = [region(big, 4096 * i, 4096).rearrange("p (c n) -> p c n", c=DC) for i in range(3)]
        at = [12288]

        def place(n):
            a = at[0]
            at[0] += n
            assert at[0] <= 32768, at[0]
            return region(big, a, n)

        QT = place(1024).rearrange("p (q t) -> p q t", q=PAIRS)
        KT = place(1024).rearrange("p (q t) -> p q t", q=PAIRS)
        QI = place(1024).rearrange("p (q t) -> p q t", q=PAIRS)
        KI = place(1024).rearrange("p (b f) -> p b f", b=NB)
        mix_row = place(1024)
        wup = place(256)[0:GATE_RANK, :]
        wra = place(128).rearrange("p (c n) -> p c n", c=DC)
        Vf = place(2048)
        V = Vf.rearrange("p (b f) -> p b f", b=NB)
        MT = Vf.rearrange("p (c t) -> p c t", c=DC)
        SGf = place(2048)
        SG = SGf.rearrange("p (b f) -> p b f", b=NB)
        qrf = place(2048)
        QKB = qrf[:, 0:1024].rearrange("p (b f) -> p b f", b=NB)
        ROT = qrf[:, 1024:2048].rearrange("p (b f) -> p b f", b=NB)
        SQ = qrf
        ST = place(1024).rearrange("p (b h i) -> p b h i", b=NB, h=HEADS)
        STATE = place(1536).rearrange("p (n q e) -> p n q e", n=3, q=PAIRS)
        Of = place(2048)
        O = Of.rearrange("p (b f) -> p b f", b=NB)
        gz, ge, gl, gg, gd = [place(512) for _ in range(5)]
        raT = place(256)[0:GATE_RANK, :]
        trig = [place(64) for _ in range(6)]
        qraw = place(512).rearrange("p (q t) -> p q t", q=2)
        kraw = place(512).rearrange("p (q t) -> p q t", q=2)
        wout0 = [w.rearrange("p c n -> p (c n)").rearrange("p (c n) -> p c n", c=4) for w in wring[0:2]]

        wout1 = [raw[:, :].rearrange("p (c n) -> p c n", c=4), region(big, 8192, 4096).rearrange("p (c n) -> p c n", c=4)]
        cosE = region(big, 0, 4096).rearrange("p (j t) -> p j t", j=S5_TILES)
        VS = region(big, 4096, 4096)
        YS = region(big, 8192, 4096)
        ANG = region(big, 12800, 4096)
        sinE = ANG.rearrange("p (j t) -> p j t", j=S5_TILES)
        wodd = region(big, 16896, 8192).rearrange("p (c n) -> p c n", c=DC)
        WS = region(big, 16896, 4096)
        wglu = region(big, 20992, 2048).rearrange("p (c n) -> p c n", c=4)
        wpool = region(big, 23040, 512).rearrange("p (g n) -> p g n", g=4)
        PM = region(big, 23552, 1024).rearrange("p (c t) -> p c t", c=4)
        s5b = region(big, 25088, 1024).rearrange("p (q r n) -> p q r n", q=4, r=2)
        s5c = region(big, 26112, 1024).rearrange("p (r j n) -> p r j n", r=2, j=S5_TILES)
        s5d = region(big, 27136, 1024).rearrange("p (r j n) -> p r j n", r=2, j=S5_TILES)
        s5t = region(big, 28160, 512).rearrange("p (j n) -> p j n", n=32)
        MT1 = region(big, 28672, 2048).rearrange("p (c t) -> p c t", c=DC)
        INV = MT1[:, 4:8, :]
        UC = region(big, 30720, 1024).rearrange("p (c t) -> p c t", c=4)
        UD = region(big, 31744, 1024).rearrange("p (c t) -> p c t", c=4)
        P1, P2 = xnT[:, 0:4, :], xnT[:, 4:8, :]
        Z, SGL = UD, P2
        v4, y4, w4 = [a.rearrange("p (r j t) -> p r j t", r=2, j=8) for a in (VS, YS, WS)]
        sine_part = [region(big, a, 512).rearrange("p (r t) -> p r t", r=2) for a in (12288, 28160)]

        wq = [[region(big, a, 4096).rearrange("p (c n) -> p c n", c=DC) for a in places]
              for places in ((8192, 12288, 0, 4096), (0, 12288, 4096, 20480))]
        qT = region(big, 16384, 4096).rearrange("p (g t) -> p g t", g=HP)
        SC = region(big, 20480, 4096).rearrange("p (b g k) -> p b g k", b=NB, g=HP)
        keysT = region(big, 24576, 2048).rearrange("p (g k) -> p g k", g=HP)
        CAND = region(big, 26624, 2048).rearrange("p (h c) -> p h c", h=PH)
        EQ = region(big, 28672, 2048)
        tk = [region(big, 30720 + 256 * i, 256) for i in range(8)]
        W = big[:, :].rearrange("p (b t) -> p b t", t=SEQ)

        gparts = [[halves[:, 4096 + 2048 * i + 1024 * k:5120 + 2048 * i + 1024 * k] for k in range(2)] for i in range(2)]

        def wq_tile(layer, m):
            return wq[layer][m // 4][:, :, P * (m % 4):P * (m % 4) + P]

        OH1 = xnT[:, :, :].rearrange("p c t -> p (c t)").rearrange("p (b t k) -> p b t k", b=4, t=4)
        OH2 = halves[:, 4096:6144].rearrange("p (b t k) -> p b t k", b=4, t=4)
        PF = [xnT[:, i, :] for i in range(2)]
        xh = halves[:, 0:2048].rearrange("p (c t) -> p c t", c=DC)
        xl = halves[:, 2048:4096].rearrange("p (c t) -> p c t", c=DC)
        uh, ul, vh, vl = [[halves[:, 4096 + 1024 * k + 512 * i:4608 + 1024 * k + 512 * i] for i in range(2)]
                          for k in range(4)]
        qparts = [[halves[:, 4096 + 2048 * i + 1024 * k:5120 + 2048 * i + 1024 * k].rearrange("p (c n) -> p c n", c=DC)
                   for k in range(2)] for i in range(2)]
        ph, pl = [[halves[:, 8192 + 512 * k + 256 * i:8448 + 512 * k + 256 * i] for i in range(2)] for k in range(2)]
        halves_of = [(uh, ul), (vh, vl)]
        slot = [raw[:, 1024 * i:1024 * i + 1024] for i in range(4)]
        assert AHEAD % 4 == 0
        LOADS = AHEAD // 4 * 2 + (NKEYS - AHEAD) // 2

        wgate = region(big, 0, 8192).rearrange("p (c n) -> p c n", c=DC)
        wple = region(big, 8192, 2048).rearrange("p (c n) -> p c n", c=2)
        pTs = region(big, 10240, 512).rearrange("p (c t) -> p c t", c=2)
        EMB = region(big, 30720, 2048).rearrange("p (b f) -> p b f", b=NB)
        GT = region(big, 10752, 2048).rearrange("p (b f) -> p b f", b=NB)

        def sm(i, n):
            return small[:, i:i + n]

        def over_b(eng, body, start, stop, n=2):
            turns = (stop - start) // n
            with eng.Fori(0, turns) as it:
                for k in range(n):
                    body(it * n + (start + k), it + (start + k) // n, (start + k) % n)
            for b in range(start + turns * n, stop):
                body(b, b // n, b % n)

        def after(eng, s, value):
            if not isinstance(value, int) or value > 0:
                eng.wait_ge(s, value)

        block = ctx.enter_context(nc.Block())

        @block.sync
        def _(sp):
            sp.dma_start(h[:, :, :], x).then_inc(s_x, 16)
            sp.dma_start(cst[:, :], consts).then_inc(s_const, 16)
            sp.dma_start(col[:, :], cols).then_inc(s_const, 16)
            sp.dma_start(posi[:, :], pos).then_inc(s_const, 16)
            sp.dma_start(wra, w_ra).then_inc(s_wra, 16)
            sp.dma_start(wup, w_up).then_inc(s_up, 16)
            for g in range(3):
                sp.dma_start(wring[g], w_even[g]).then_inc(s_win[g], 16)
            sp.dma_start(mix_row, rows[:, 0:D]).then_inc(s_row, 16)
            for g in range(3, 6):
                sp.wait_ge(pe_out, NUMBER[("kaT", "va.1", "ga.1")[g - 3]] + 1)
                sp.dma_start(wring[g % 3], w_even[g]).then_inc(s_win[g % 3], 16)
            for i in range(2):
                sp.wait_ge(pe_out, NUMBER[("qkb.1", "vb.1")[i]] + 1)
                sp.dma_start(wout0[i], w_out0[:, 4 * i:4 * i + 4, :]).then_inc(s_wout, 16)

            def load_wq(layer, g):
                sp.dma_start(wq[layer][g], w_q[layer, g]).then_inc(s_wq[g], 16)

            sp.wait_ge(pe_out, NUMBER["gb.1"] + 1)
            load_wq(0, 0)
            sp.wait_ge(pe_out, NUMBER["o.3"] + 1)
            load_wq(0, 1)
            for layer in range(DEPTH):
                if layer:
                    sp.wait_ge(s_ul, 2 * NKEYS)
                    sp.wait_ge(s_vl, 2 * NKEYS)
                    sp.dma_start(wout1[0], w_out1[:, 0:4, :]).then_inc(s_wout, 16)
                    sp.wait_ge(pe_out, NUMBER["xnT3.3"] + 1)
                    sp.dma_start(INV, counts).then_inc(s_counts, 16)
                    sp.wait_ge(pe_out, NUMBER["ucT.1"] + 1)
                    sp.dma_start(wpool, w_pool).then_inc(s_late, 16)
                    sp.dma_start(wglu, w_glu).then_inc(s_late, 16)
                    sp.wait_ge(s_xst, 2)
                    sp.dma_start(wout1[1], w_out1[:, 4:8, :]).then_inc(s_wout, 16)
                    load_wq(1, 0)
                    load_wq(1, 1)
                    sp.wait_ge(pe_out, NUMBER["ys.1"] + 1)
                    load_wq(1, 2)
                    sp.wait_ge(pe_out, NUMBER["glu.1"] + 1)
                    load_wq(1, 3)
                else:
                    sp.wait_ge(pe_out, NUMBER["mix0.3"] + 1)
                    load_wq(0, 2)
                    load_wq(0, 3)
                sp.dma_start(keysT, keys[layer]).then_inc(s_keys, 16)
                sp.wait_ge(pe_out, NUMBER[f"mix{layer}.3"] + 1)
                b0 = NKEYS * layer

                def load(table, b, k, written, count):
                    after(sp, written, count)
                    sp.dma_start(slot[k], table[layer, bass.ds(b, 1)].rearrange("o p n -> p (o n)")).then_inc(s_raw[k], 16)

                def load_u(b, s):
                    load(u_tab, b, s, s_ul, b * 2 + (2 * b0 - 2))

                def load_v(b, s):
                    load(v_tab, b, 2 + s, s_vl, b * 2 + (2 * b0 - 2))

                def load_both(b, h_, s):
                    load_u(b + 1, 1 - s)
                    load_v(b, s)

                for b in range(4):
                    load(u_tab, b, b, s_ul, 0)
                over_b(sp, lambda b, h_, k: load(u_tab, b, k, s_ul, b * 2 + (2 * b0 - 6)), 4, AHEAD, 4)
                for b in range(4):
                    load(v_tab, b, b, s_ul, 2 * b0 + 2 * (AHEAD - 4 + b + 1))
                over_b(sp, lambda b, h_, k: load(v_tab, b, k, s_vl, b * 2 + (2 * b0 - 6)), 4, AHEAD, 4)
                load(u_tab, AHEAD, 0, s_vl, 2 * b0 + 2 * (AHEAD - 3))
                load(u_tab, AHEAD + 1, 1, s_vl, 2 * b0 + 2 * (AHEAD - 2))
                load(v_tab, AHEAD, 2, s_vl, 2 * b0 + 2 * (AHEAD - 1))
                load_u(AHEAD + 2, 0)
                load(v_tab, AHEAD + 1, 3, s_vl, 2 * b0 + 2 * AHEAD)

                def load_and_ple(b, q, k):
                    load_both(b, None, k % 2)
                    if k == 0:
                        sp.dma_start(big[:, bass.ds((q - PLE_FROM // 4) * D, D)],
                                     w_ple[layer, bass.ds(q - PLE_FROM // 4, 1)].rearrange("o p n -> p (o n)")
                                     ).then_inc(s_ple, 16)

                def load_and_odd(b, h_, s):
                    load_both(b, h_, s)
                    if s == 0:
                        sp.dma_start(big[:, bass.ds((h_ - ODD_FROM // 2) * D + 16896, D)],
                                     w_odd[bass.ds(h_ - ODD_FROM // 2, 1)].rearrange("o p n -> p (o n)")
                                     ).then_inc(s_odd, 16)

                over_b(sp, load_both, AHEAD + 2, PLE_FROM)
                over_b(sp, load_and_ple, PLE_FROM, PLE_FROM + 40, 4)
                sp.dma_start(pTs, pT[layer]).then_inc(s_ple, 16)
                if layer == 0:
                    over_b(sp, load_both, PLE_FROM + 40, ODD_FROM)
                    over_b(sp, load_and_odd, ODD_FROM, ODD_FROM + 16)
                    sp.dma_start(s5c, s5_c).then_inc(s_s5, 16)
                    load_both(ODD_FROM + 16, None, 0)
                    sp.dma_start(s5b, s5_b).then_inc(s_s5, 16)
                    over_b(sp, load_both, ODD_FROM + 17, NKEYS - 1)
                else:
                    over_b(sp, load_both, PLE_FROM + 40, NKEYS - 1)
                load_v(NKEYS - 1, 1)
            sp.dma_start(final_row, rows[:, D:2 * D]).then_inc(s_row, 16)
            sp.wait_ge(s_fin, 2)
            sp.dma_start(out, xs).then_inc(s_out, 16)
            sp.wait_ge(s_out, 16)

        @block.tensor
        def _(pe):
            def emit(name, ins):
                ins.then_inc(pe_out, 1)

            def transpose_norm(site):
                for i in range(4):
                    B, c0 = i // 2, 4 * (i % 2)
                    pe.wait_ge(s_xs[B], site + 1)
                    o = output(pe, f"xnT{site}.{i}")
                    for c in range(4):
                        last = pe.transpose(o[:, c * P:(c + 1) * P], xs[:, B, (c0 + c) * P:(c0 + c + 1) * P], ident)
                    emit(f"xnT{site}.{i}", last)
                ready(pe, f"xnT{site}.3")

            def product(o, pairs):
                for i, (a, b) in enumerate(pairs):
                    last = pe.matmul(o, a, b, start=(i == 0), stop=(i == len(pairs) - 1))
                return last

            def tokens_by(name, lhs, rhs, n=DC):
                for i in range(4):
                    B, hf = i // 2, i % 2
                    o = output(pe, f"{name}.{i}")
                    emit(name, product(o[:, :], [(lhs[:, c, B * P:(B + 1) * P], rhs(c)[:, 512 * hf:512 * hf + 512])
                                                 for c in range(n)]))

            pe.wait_ge(s_const, 48)
            transpose_norm(0)
            pe.wait_ge(s_win[0], 16)
            for m, name in enumerate(("qaT", "kaT")):
                o = output(pe, name)
                for q in range(2):
                    f = 256 * m + P * q
                    last = product(o[:, 256 * q:256 * q + 256], [(wring[0][:, c, f:f + P], xnT[:, c, :]) for c in range(DC)])
                emit(name, last)
            pe.wait_ge(s_wra, 16)
            o = output(pe, "raT")
            emit("raT", product(o[0:GATE_RANK, 0:SEQ], [(wra[:, c, :], xnT[:, c, :]) for c in range(DC)]))
            pe.wait_ge(s_up, 16)
            ready(pe, "raT")
            o = output(pe, "zT")
            for q in range(2):
                last = pe.matmul(o[:, 256 * q:256 * q + 256], wup[:, P * q:P * q + P], raT, start=True, stop=True)
            emit("zT", last)
            for g, name in enumerate(("va", "ga", "qkb", "vb", "gb"), start=1):
                pe.wait_ge(s_win[g % 3], 16 * (g // 3 + 1))
                for B in range(NB):
                    o = output(pe, f"{name}.{B}")
                    last = product(o[:, :], [(xnT[:, c, B * P:(B + 1) * P], wring[g % 3][:, c, :]) for c in range(DC)])
                    emit(name, last)
            pe.wait_ge(s_rot, 2)
            for m, name in enumerate(("rqT", "rkT")):
                o = output(pe, name)
                for q in range(2):
                    for B in range(NB):
                        f = 256 * m + P * q
                        last = pe.transpose(o[:, 256 * q + P * B:256 * q + P * B + P], ROT[:, B, f:f + P], ident)
                emit(name, last)
            pe.wait_ge(s_qt, 4)
            o = output(pe, "kgT")
            for B in range(NB):
                for q in range(2):
                    last = pe.transpose(o[:, 256 * B + P * q:256 * B + P * q + P], kraw[:, q, B * P:(B + 1) * P], ident)
            emit("kgT", last)
            ready(pe, "rkT")
            for B in range(NB):
                o = output(pe, f"sT.{B}")
                for odd in range(2):
                    for p in range(2):
                        for hh in range(odd, HEADS, 2):
                            r, t0 = HD * odd, B * P + CHUNK * p
                            last = pe.matmul(o[HD * p:HD * p + HD, 64 * hh:64 * hh + 64],
                                             KT[r:r + HD, hh // 2, t0:t0 + CHUNK], QT[r:r + HD, hh // 2, t0:t0 + CHUNK],
                                             start=True, stop=True)
                    if not odd:
                        done(pe, last, s_rows)
                emit("sT", last)
            ready(pe, "kgT")
            pe.wait_ge(s_ret, 3)
            for n in range(3):
                o = output(pe, f"kv.{n}")
                B, r = n // 2, CHUNK * (n % 2)
                for hh in range(HEADS):
                    q, d0 = hh // 2, HD * (hh % 2)
                    last = pe.matmul(o[d0:d0 + HD, P * q:P * q + P], KI[r:r + CHUNK, B, HD * hh:HD * hh + HD],
                                     V[r:r + CHUNK, B, P * hh:P * hh + P], start=True, stop=True)
                emit("kv", last)
            pe.wait_ge(s_masked_v, 2)
            pe.wait_ge(s_masked_p, 4)
            ready(pe, "kv.2")
            for i in range(4):
                B, hf = i // 2, i % 2
                o = output(pe, f"o.{i}")
                heads = range(4 * hf, 4 * hf + 4)

                def dst(p, hh):
                    return o[CHUNK * p:CHUNK * p + CHUNK, P * (hh % 4):P * (hh % 4) + P]

                for p in range(2):
                    for hh in heads:
                        last = pe.matmul(dst(p, hh), ST[CHUNK * p:CHUNK * p + CHUNK, B, hh, :],
                                         V[CHUNK * p:CHUNK * p + CHUNK, B, P * hh:P * hh + P],
                                         start=(hh == heads[0]), stop=False, skip_group_check=True)
                for other in range(2):
                    if other:
                        done(pe, last, s_rows)
                    for p in range(2):
                        n = 2 * B + p
                        for hh in heads:
                            if n and (hh + p) % 2 == other:
                                r, t0 = HD * (hh % 2), CHUNK * n
                                last = pe.matmul(dst(p, hh), QI[r:r + HD, hh // 2, t0:t0 + CHUNK],
                                                 STATE[r:r + HD, n - 1, hh // 2, :], start=False, stop=True,
                                                 skip_group_check=True)
                emit("o", last)
            for i in range(4):
                B, c0 = i // 2, 4 * (i % 2)
                pe.wait_ge(s_oready, B + 1)
                o = output(pe, f"oT.{i}")
                for c in range(4):
                    last = pe.transpose(o[:, c * P:(c + 1) * P], O[:, B, (c0 + c) * P:(c0 + c + 1) * P], ident)
                emit("oT", last)
            ready(pe, "oT.3")
            pe.wait_ge(s_wout, 32)
            tokens_by("mix0", MT, lambda c: wout0[c // 4][:, c % 4, :])

            for layer in range(DEPTH):
                if layer:
                    transpose_norm(3)
                    pe.wait_ge(s_odd, 16 * DC)

                    def odd_in(name, first):
                        for m in range(2):
                            o = output(pe, f"{name}.{m}")
                            for q in range(2):
                                f = first + 256 * m + P * q
                                last = product(o[:, 256 * q:256 * q + 256],
                                               [(wodd[:, c, f:f + P], xnT[:, c, :]) for c in range(DC)])
                            emit(name, last)

                    odd_in("udT", 512)
                    pe.wait_ge(s_s5, 32)
                    ready(pe, "udT.1")
                    for half in range(2):
                        for j in range(8 * half, 8 * half + 8):
                            o = output(pe, f"bu.{j}")
                            r, q = 32 * (j % 4), j // 4
                            for ri in range(2):
                                last = pe.matmul(o[:, 256 * ri:256 * ri + 256], s5b[r:r + 32, q, ri, :], UD[r:r + 32, q, :],
                                                 start=True, stop=True)
                            emit("bu", last)
                        if half == 0:
                            odd_in("ucT", 0)
                        else:
                            pe.wait_ge(s_late, 32)
                            pe.wait_ge(s_pool, 1)
                            for m in range(2):
                                o = output(pe, f"pmT.{m}")
                                for q in range(2):
                                    last = pe.matmul(o[:, 256 * q:256 * q + 256], wpool[:, 2 * m + q, :], PM[:, 2 * m + q, :],
                                                     start=True, stop=True)
                                emit("pmT", last)
                            ready(pe, "pmT.1")
                            pe.wait_ge(s_wout, 48)
                            tokens_by("mixp", MT1, lambda c: wout1[0][:, c, :], n=4)
                        pe.wait_ge(s_xst, half + 1)
                        pe.wait_ge(s_c, 1)
                        o = output(pe, f"ys.{half}")
                        xst = VS.rearrange("p (r j t) -> p r j t", r=2, j=8)
                        for q in range(2):
                            for jj in range(4):
                                j = 4 * q + jj
                                for ri in range(2):
                                    last = pe.matmul(o[32 * jj:32 * jj + 32, 256 * q:256 * q + 256],
                                                     s5d[:, ri, 8 * half + j, :], xst[:, ri, j, :],
                                                     start=(ri == 0), stop=(ri == 1))
                        emit("ys", last)
                    pe.wait_ge(s_z, 1)
                    for m in range(2):
                        o = output(pe, f"glu.{m}")
                        for q in range(2):
                            f = 256 * m + P * q
                            last = product(o[:, 256 * q:256 * q + 256], [(wglu[:, c, f:f + P], Z[:, c, :]) for c in range(4)])
                        emit("glu", last)
                    pe.wait_ge(s_mt, 1)
                    pe.wait_ge(s_wout, 64)
                    tokens_by("mix1", MT1[:, 4:8, :], lambda c: wout1[1][:, c, :], n=4)

                transpose_norm(1 + 3 * layer)
                pe.wait_ge(s_xl, 4 * SPLIT.index(1 + 3 * layer) + 4)
                for i in range(8):
                    o = output(pe, f"q{layer}.{i}")
                    for q in range(2):
                        m = 2 * i + q
                        pe.wait_ge(s_ql, HP * layer + m + 1)
                        w_hi, w_lo = qparts[m % 2]
                        last = product(o[:, 256 * q:256 * q + 256],
                                       [pair for c in range(DC) for pair in
                                        ((w_lo[:, c, :], xh[:, c, :]), (w_hi[:, c, :], xl[:, c, :]),
                                         (w_hi[:, c, :], xh[:, c, :]))])
                        if q == 0:
                            last.then_inc(s_qused, 1)
                    emit("q", last)
                pe.wait_ge(s_keys, 16 * (layer + 1))
                ready(pe, f"q{layer}.7")
                for i in range(8):
                    B, g0 = i // 4, 4 * (i % 4)
                    o = output(pe, f"scores{layer}.{i}")
                    for g in range(4):
                        last = pe.matmul(o[:, P * g:P * g + P], qT[:, g0 + g, B * P:(B + 1) * P], keysT[:, g0 + g, :],
                                         start=True, stop=True)
                    emit("scores", last)
                b0 = NKEYS * layer

                def hidden(b, s, bank_free, hi=uh, lo=ul):
                    after(pe, bank_free, b + (b0 - 1))
                    for half in range(2):
                        pe.wait_ge(s_ul, b * 2 + (2 * b0 + half + 1))
                        for c in range(4):
                            u_hi, u_lo = [u[half][:, c * P:(c + 1) * P] for u in (hi, lo)]
                            x_hi, x_lo = xh[:, 4 * half + c, :], xl[:, 4 * half + c, :]
                            pe.matmul(work[s][:, 0:SEQ], u_lo, x_hi, start=(half == 0 and c == 0), stop=False)
                            pe.matmul(work[s][:, 0:SEQ], u_hi, x_lo, start=False, stop=False)
                            last = pe.matmul(work[s][:, 0:SEQ], u_hi, x_hi, start=False, stop=(half == 1 and c == 3))
                        last.then_inc(s_uused, 1)

                def gated(b, s, first=False, final=False, hi=vh, lo=vl):
                    pe.wait_ge(s_p, b + (b0 + 1))
                    for hf in range(2):
                        pe.wait_ge(s_vl, b * 2 + (2 * b0 + hf + 1))
                        for B in range(NB):
                            acc = sums[2 * B + hf][:, :]
                            p_hi, p_lo = [x[s][:, B * P:(B + 1) * P] for x in (ph, pl)]
                            pe.matmul(acc, p_lo, hi[hf], start=first, stop=False, skip_group_check=True)
                            pe.matmul(acc, p_hi, lo[hf], start=False, stop=False, skip_group_check=True)
                            last = pe.matmul(acc, p_hi, hi[hf], start=False, stop=final, skip_group_check=True)
                        last.then_inc(s_vused, 1)

                ready(pe, f"scores{layer}.7")
                for b in range(2):
                    hidden(b, b, s_gelu, *halves_of[b])
                over_b(pe, lambda b, h_, s: hidden(b, s, s_gelu, *halves_of[s]), 2, AHEAD)
                pe.wait_ge(s_gelu, b0 + AHEAD)
                for B in range(NB):
                    pe.wait_ge(s_route, NB * layer + B + 1)
                    o = output(pe, f"routes{layer}.{B}")
                    for k in range(3):
                        last = pe.transpose(o[:, P * k:P * k + P], tk[5 + k][:, P * B:P * B + P], ident)
                    emit("routes", last)
                ready(pe, f"routes{layer}.1")

                def gate_group(g, k, first):
                    for rows_ready in (s_first, s_second):
                        pe.wait_ge(rows_ready, g + (NG * layer + 1))
                    if not first:
                        pe.wait_ge(s_wmul, g + (NG * layer - 3))
                    for t in range(4):
                        last = pe.matmul(work[k][:, P * t:P * t + P], OH1[:, k, t, :], OH2[:, k, t, :].bitcast(F32),
                                         start=True, stop=True)
                    last.then_inc(s_wps, 1)

                for g in range(4):
                    gate_group(g, g, True)
                with pe.Fori(1, NG // 4) as it:
                    for k in range(4):
                        gate_group(it * 4 + k, k, False)
                pe.wait_ge(s_wmul, NG * (layer + 1))
                gated(0, 0, True, False, *halves_of[0])
                over_b(pe, lambda b, h_, s: gated(b, s, False, False, *halves_of[s]), 1, AHEAD - 1)

                def both(b, h_, s):
                    hidden(b + 1, 1 - s, s_p)
                    gated(b, s)

                both(AHEAD - 1, None, (AHEAD - 1) % 2)
                over_b(pe, both, AHEAD, NKEYS - 1)
                gated(NKEYS - 1, 1, final=True)

                pe.wait_ge(s_ple, 16 * 11 * (layer + 1))
                tokens_by(f"ple{layer}", pTs, lambda c: wple[:, c, :], n=2)
                transpose_norm(2 + 3 * layer)
                pe.wait_ge(s_xl, 4 * SPLIT.index(2 + 3 * layer) + 4)
                gates = [output(pe, f"gate{layer}.{i}") for i in range(4)]
                for c in range(DC):
                    pe.wait_ge(s_gl, DC * layer + c + 1)
                    w_hi, w_lo = gparts[c % 2]
                    for i in range(4):
                        B, cols_ = i // 2, slice(512 * (i % 2), 512 * (i % 2) + 512)
                        x_hi, x_lo = [a[:, c, B * P:B * P + P] for a in (xh, xl)]
                        pe.matmul(gates[i][:, :], x_hi, w_lo[:, cols_], start=(c == 0), stop=False)
                        pe.matmul(gates[i][:, :], x_lo, w_hi[:, cols_], start=False, stop=False)
                        last = pe.matmul(gates[i][:, :], x_hi, w_hi[:, cols_], start=False, stop=(c == DC - 1))
                        if c == DC - 1:
                            emit(f"gate{layer}.{i}", last)
                    if c < DC - 1:
                        last.then_inc(s_gused, 1)

        @block.scalar
        def _(act):
            def step(ins):
                done(act, ins, a_step)

            def copy_out(name, dst, src=None, func=ACT.Copy, **kw):
                o = arrive(act, name)
                took(act, act.activation(dst, (o[:, :] if src is None else src(o)), func, **kw), "act")

            def norm_rstd(site):
                act.preload_act_table(ACT.Sqrt)
                if site == 0:
                    act.wait_ge(s_x, 16)
                elif site % 3 == 2:
                    act.wait_ge(s_added, site // 3 + 1)
                else:
                    if site % 3:
                        ready(act, f"mix{site // 3}.3")
                    else:
                        act.wait_ge(s_emb, site // 3)
                act.activation(xs[:, 1, :], h[:, 1, :], ACT.Square, accum_out=sm(1, 1)).then_inc(s_square, 1)
                act.wait_ge(s_var, site + 1)
                done(act, act.activation(sm(4, 2), sm(2, 2), ACT.Sqrt), s_rstd)
                if site < 6:
                    act.activation(xs[:, 1, :], h[:, 1, :], ACT.Copy, scale=sm(5, 1)).then_inc(s_xs[1], 1)

            def x_high(site):
                for i in range(4):
                    B, c0 = i // 2, 4 * (i % 2)
                    ready(act, f"xnT{site}.{i}")
                    act.activation(xh[:, c0:c0 + 4, B * P:(B + 1) * P], xnT[:, c0:c0 + 4, B * P:(B + 1) * P],
                                   ACT.Copy).then_inc(s_xh, 1)

            norm_rstd(0)
            act.wait_ge(s_rope_ang, 1)
            act.activation(trig[2], trig[0], ACT.Sin).then_inc(s_rope_sin, 1)
            act.activation(trig[3], trig[0], ACT.Sin, scale=0.5).then_inc(s_rope_sin, 1)
            copy_out("qaT", qraw.rearrange("p q t -> p (q t)"), scale=HD ** -0.5)
            copy_out("kaT", kraw.rearrange("p q t -> p (q t)"))
            copy_out("raT", raT, lambda o: o[0:GATE_RANK, 0:SEQ])
            act.wait_ge(s_log, 1)
            step(act.activation(ge, ge, ACT.Exp, scale=-1.0))
            done(act, act.activation(gl, ge, ACT.Ln, bias=1.0), s_loga)
            for B in range(NB):
                copy_out(f"va.{B}", V[:, B, 0:512])
            for B in range(NB):
                copy_out(f"ga.{B}", SG[:, B, 0:512])
            act.wait_ge(s_gd, 3)
            act.activation(gl, gd, ACT.Exp).then_inc(s_ge, 1)
            act.activation(gz, gd, ACT.Exp, scale=-1.0).then_inc(s_ge, 1)
            act.activation(ge, ge, ACT.Exp).then_inc(s_ge, 1)
            act.activation(sm(16, 8), gg.rearrange("p (q n i) -> p (q n) i", q=2, i=CHUNK)[:, :, CHUNK - 1],
                           ACT.Exp).then_inc(s_ge, 1)
            act.wait_ge(s_ge, 4)
            act.activation(gg, gg, ACT.Exp).then_inc(s_ge, 1)
            act.wait_ge(s_const, 48)
            done(act, act.activation(sm(100, 16), K("ldt"), ACT.Exp), s_par_a)
            act.wait_ge(s_par_v, 2)
            done(act, act.activation(sm(148, 16), sm(116, 16), ACT.Exp), s_par_a)
            act.wait_ge(s_par_v, 3)
            done(act, act.activation(sm(164, 16), sm(132, 16), ACT.Sin), s_par_a)
            done(act, act.activation(sm(180, 16), sm(132, 16), ACT.Sin, scale=0.5), s_par_a)
            for name in ("qkb", "vb", "gb"):
                for B in range(NB):
                    dst = {"qkb": QKB[:, B, :], "vb": V[:, B, 512:1024], "gb": SG[:, B, 512:1024]}[name]
                    copy_out(f"{name}.{B}", dst)
            done(act, act.activation(SGf, SGf, ACT.Silu), s_silu)
            copy_out("rqT", QT[:, 2:4, :].rearrange("p q t -> p (q t)"))
            copy_out("rkT", KT[:, 2:4, :].rearrange("p q t -> p (q t)"))
            o = arrive(act, "kgT")
            took(act, act.activation(KI[:, :, 0:256], o[:, :].rearrange("p (b f) -> p b f", b=NB), ACT.Copy), "act")
            for B in range(NB):
                copy_out(f"sT.{B}", ST[:, B, :, :].rearrange("p h i -> p (h i)"))
            for i in range(4):
                copy_out(f"o.{i}", O[:, i // 2, 512 * (i % 2):512 * (i % 2) + 512])
            for B in range(NB):
                act.wait_ge(s_cen, B + 1)
                done(act, act.activation(SQ[:, D * B:D * B + D], Of[:, D * B:D * B + D], ACT.Square), s_sq)
            act.wait_ge(s_hvar, 1)
            done(act, act.activation(sm(40, 16), sm(24, 16), ACT.Sqrt), s_hrstd)
            for i in range(4):
                B, c0 = i // 2, 4 * (i % 2)
                o = arrive(act, f"oT.{i}")
                took(act, act.activation(MT[:, c0:c0 + 4, B * P:(B + 1) * P],
                                         o[:, :].rearrange("p (c t) -> p c t", c=4), ACT.Copy), "act")

            for layer in range(DEPTH):
                if layer:
                    norm_rstd(3)
                    done(act, act.activation(cosE.rearrange("p j t -> p (j t)"), ANG, ACT.Sin, scale=0.5), s_sin)
                    done(act, act.activation(ANG, ANG, ACT.Sin), s_sin)
                    for m in range(2):
                        copy_out(f"udT.{m}", UD[:, 2 * m:2 * m + 2, :].rearrange("p c t -> p (c t)"))
                    for m in range(2):
                        copy_out(f"ucT.{m}", UC[:, 2 * m:2 * m + 2, :].rearrange("p c t -> p (c t)"))
                    for m in range(2):
                        o = arrive(act, f"pmT.{m}")
                        step(act.activation(MT1[:, 2 * m, :], o[:, 0:256], ACT.Copy, scale=K("pscale", 2 * m, 1)))
                        took(act, act.activation(MT1[:, 2 * m + 1, :], o[:, 256:512], ACT.Copy,
                                                 scale=K("pscale", 2 * m + 1, 1)), "act")
                    ready(act, "ys.1")
                    done(act, act.activation(Z, Z, ACT.Gelu), s_z)
                    for m in range(2):
                        o = arrive(act, f"glu.{m}")
                        for q in range(2):
                            ins = act.activation(SGL[:, 2 * m + q, :], o[:, 256 * q:256 * q + 256], ACT.Sigmoid,
                                                 bias=K("bglu", 2 * m + q, 1))
                            if q:
                                took(act, ins, "act")
                            else:
                                step(ins)


                def q_high(m):
                    act.wait_ge(s_wq[m // 4], 16 * (layer + 1))
                    if m >= 2:
                        if m % 2 == 0:
                            act.wait_ge(s_qused, PH * layer + m // 2)
                        else:
                            act.wait_ge(pe_out, NUMBER[f"q{layer}.{m // 2 - 1}"] + 1)
                    act.activation(qparts[m % 2][0], wq_tile(layer, m), ACT.Copy).then_inc(s_qh, 1)

                for m in range(2):
                    q_high(m)
                norm_rstd(1 + 3 * layer)
                x_high(1 + 3 * layer)
                for i in range(8):
                    for m in (2 * i + 2, 2 * i + 3):
                        if m < HP:
                            q_high(m)
                    copy_out(f"q{layer}.{i}", qT[:, 2 * i:2 * i + 2, :].rearrange("p g t -> p (g t)"))
                for i in range(8):
                    B, g0 = i // 4, 4 * (i % 4)
                    copy_out(f"scores{layer}.{i}", SC[:, B, g0:g0 + 4, :].rearrange("p g k -> p (g k)"))
                b0 = NKEYS * layer

                def high(b, k, turn, parts, signal, used, back):
                    act.wait_ge(s_raw[k], turn * 16 + 16 * (LOADS * layer + 1))
                    for half in range(2):
                        after(act, used, b * 2 + (2 * b0 + half + 1 - 2 * back))
                        act.activation(parts[half], slot[k][:, 512 * half:512 * half + 512], ACT.Copy).then_inc(signal, 1)

                def high_u_ahead(b, q, k):
                    high(b, k, q, halves_of[k % 2][0], s_uh, s_uused, 2)

                def high_v_ahead(b, q, k):
                    high(b, k, q + AHEAD // 4, halves_of[k % 2][0], s_vh, s_vused, 2)

                def high_u(b, h_, s):
                    high(b, s, h_, uh, s_uh, s_uused, 1)

                def high_v(b, h_, s):
                    high(b, 2 + s, h_, vh, s_vh, s_vused, 1)

                def gelu(b, s, dst):
                    act.wait_ge(s_uused, b * 2 + (2 * b0 + 2))
                    act.activation(dst, work[s][:, 0:SEQ], ACT.Gelu).then_inc(s_gelu, 1)

                def ahead(b, q, k):
                    high_u_ahead(b + 1, q + (k + 1) // 4, (k + 1) % 4)
                    gelu(b, k % 2, big[:, bass.ds(b * SEQ, SEQ)])

                act.wait_ge(pe_out, NUMBER[f"q{layer}.7"] + 1)
                act.preload_act_table(ACT.Gelu)
                high_u_ahead(0, 0, 0)
                for b in range(2):
                    ahead(b, 0, b)
                over_b(act, ahead, 2, AHEAD - 1, 4)
                gelu(AHEAD - 1, (AHEAD - 1) % 2, big[:, (AHEAD - 1) * SEQ:AHEAD * SEQ])
                act.wait_ge(s_best, NB * (layer + 1))
                done(act, act.activation(tk[4], tk[4], ACT.Exp), s_exp)
                for B in range(NB):
                    o = arrive(act, f"routes{layer}.{B}")
                    took(act, act.activation(routesT[:, :, B * P:(B + 1) * P],
                                             o[:, 0:384].rearrange("p (k t) -> p k t", k=3), ACT.Copy), "act")
                def second_rows(g, k, before):
                    rows_ = OH2[:, k % 4, :, :]
                    act.wait_ge(s_far, g + (NG * layer + 1))
                    act.activation(rows_, rows_.bitcast(F32), ACT.Abs).then_inc(s_near, 1)
                    if before:
                        act.wait_ge(s_wps, g + (NG * layer - 1))
                        gates_out(g - 2, (k - 2) % 4)
                    act.wait_ge(s_near, g + (NG * layer + 1))
                    act.activation(rows_, rows_.bitcast(F32), ACT.Relu, scale=-1.0, bias=1.0).then_inc(s_second, 1)

                def gates_out(g, k):
                    act.activation(W[:, AHEAD:NKEYS, bass.ds(g * 4, 4)],
                                   work[k][:, :].rearrange("p (t b) -> p b t", t=4)[:, AHEAD:NKEYS, :],
                                   ACT.Copy).then_inc(s_wsb, 1)

                for g in range(4):
                    second_rows(g, g, g >= 2)
                with act.Fori(1, NG // 4) as it:
                    for k in range(4):
                        second_rows(it * 4 + k, k, True)
                for g in range(NG - 2, NG):
                    act.wait_ge(s_wps, NG * layer + g + 1)
                    gates_out(g, g % 4)
                act.preload_act_table(ACT.Gelu)
                for b in range(2):
                    high_v_ahead(b, 0, b)
                over_b(act, high_v_ahead, 2, AHEAD - 1, 4)
                act.wait_ge(s_vused, 2 * b0 + 2 * (AHEAD - 1))
                high_u(AHEAD, AHEAD // 2, 0)
                high_v_ahead(AHEAD - 1, AHEAD // 4 - 1, 3)

                def gelu_v(b, h_, s):
                    gelu(b, s, work[s][:, 0:SEQ])
                    high_v(b, h_, s)

                def u_gelu_v(b, h_, s):
                    high_u(b + 1, h_ + s, 1 - s)
                    gelu_v(b, h_, s)

                over_b(act, u_gelu_v, AHEAD, NKEYS - 1)
                gelu_v(NKEYS - 1, NKEYS // 2 - 1, 1)

                def gate_high(c):
                    if c >= 2:
                        act.wait_ge(s_gused, (DC - 1) * layer + c - 1)
                    act.activation(gparts[c % 2][0], wgate[:, c, :], ACT.Copy).then_inc(s_gh, 1)

                act.wait_ge(s_ple, 16 * 11 * (layer + 1))
                gate_high(0)
                act.wait_ge(s_vused, 2 * NKEYS * (layer + 1))
                gate_high(1)
                norm_rstd(2 + 3 * layer)
                for i in range(4):
                    copy_out(f"ple{layer}.{i}", EMB[:, i // 2, 512 * (i % 2):512 * (i % 2) + 512])
                x_high(2 + 3 * layer)
                for c in range(2, DC):
                    gate_high(c)
                if layer == 0:
                    act.wait_ge(s_ang, 4)
                for i in range(4):
                    copy_out(f"gate{layer}.{i}", GT[:, i // 2, 512 * (i % 2):512 * (i % 2) + 512], func=ACT.Sigmoid)
            norm_rstd(6)

        @block.gpsimd
        def _(pool):
            for B in range(NB):
                ready(pool, f"sT.{B}")
                for p in range(2):
                    v = ST[CHUNK * p:CHUNK * p + CHUNK, B, 0:4, :]
                    done(pool, pool.affine_select(out=v, in_=v, compare_op=ALU.is_ge, fill=0.0, base=0,
                                                  pattern=[[0, 4], [1, CHUNK]], channel_multiplier=-1), s_masked_p)
            def step(ins):
                done(pool, ins, p_step)

            def s5_angles():
                pool.wait_ge(s_p, 66)
                pool.wait_ge(s_coef, 1)
                k, kc = region(big, 10752, 1024), region(big, 11776, 1024)
                for i in range(4):
                    a = ANG[:, 1024 * i:1024 * i + 1024]
                    step(pool.tensor_tensor(a.rearrange("p (j t) -> p j t", j=4),
                                            C("time").unsqueeze(1).to_broadcast([P, 4, SEQ]),
                                            sm(132 + 4 * i, 4).unsqueeze(2).to_broadcast([P, 4, SEQ]), ALU.mult))
                    step(pool.tensor_scalar(k, a, 1.0 / TWO_PI, ROUND, ALU.mult, ALU.add))
                    step(pool.tensor_scalar(k, k, -ROUND, None, ALU.add))
                    for c in (C1, C2, C3):
                        step(pool.tensor_scalar(kc, k, -c, None, ALU.mult))
                        step(pool.tensor_tensor(a, a, kc, ALU.add))
                    done(pool, pool.tensor_scalar(a, a, PI_LOW, -PI_LOW, ALU.min, ALU.max), s_ang)

            def s5_output_map():
                pool.wait_ge(s_p, 112)
                pool.wait_ge(s_s5, 32)
                cre, cim, ncre, ncim = [sm(i, 16).unsqueeze(2).to_broadcast([P, S5_TILES, 32])
                                        for i in (276, 292, 460, 476)]
                step(pool.tensor_tensor(s5t, s5c[:, 1, :, :], cim, ALU.mult))
                step(pool.tensor_tensor(s5d[:, 0, :, :], s5c[:, 0, :, :], cre, ALU.mult))
                step(pool.tensor_tensor(s5d[:, 0, :, :], s5d[:, 0, :, :], s5t, ALU.subtract))
                step(pool.tensor_tensor(s5t, s5c[:, 0, :, :], ncim, ALU.mult))
                step(pool.tensor_tensor(s5d[:, 1, :, :], s5c[:, 1, :, :], ncre, ALU.mult))
                done(pool, pool.tensor_tensor(s5d[:, 1, :, :], s5d[:, 1, :, :], s5t, ALU.add), s_c)

            def s5_inputs(half):
                for j in range(8):
                    pool.wait_ge(s_turned, 8 * half + j + 1)
                    ready(pool, f"bu.{8 * half + j}")
                    sine = sine_part[j % 2]
                    pool.tensor_tensor(v4[:, 0, j, :], y4[:, 0, j, :], sine[:, 1, :], ALU.add)
                    pool.tensor_tensor(v4[:, 1, j, :], y4[:, 1, j, :], sine[:, 0, :], ALU.subtract).then_inc(s_drive, 1)

            def pooling():
                ready(pool, "ucT.1")
                pool.wait_ge(s_counts, 16)
                src, dst = UC, P1
                for k, w in enumerate((1, 2, 4, 8)):
                    step(pool.tensor_copy(dst[:, k:4, 0:w], src[:, k:4, 0:w]))
                    step(pool.tensor_tensor(dst[:, k:4, w:SEQ], src[:, k:4, w:SEQ], src[:, k:4, 0:SEQ - w], ALU.add))
                    src, dst = dst, (P2 if dst is P1 else P1)
                for g in range(4):
                    s_ = P1 if g % 2 == 0 else P2
                    step(pool.tensor_tensor(PM[:, g, :], s_[:, g, :], INV[:, g, :], ALU.mult))
                done(pool, pool.tensor_tensor(PM, PM, UC, ALU.subtract), s_pool)

            for layer in range(DEPTH):

                def low_u(b, q, k):
                    hi, lo = halves_of[k % 2]
                    for half in range(2):
                        pool.wait_ge(s_uh, b * 2 + (2 * NKEYS * layer + half + 1))
                        pool.tensor_tensor(lo[half], slot[k][:, 512 * half:512 * half + 512], hi[half].bitcast(F32),
                                           ALU.subtract).then_inc(s_ul, 1)

                over_b(pool, low_u, 0, AHEAD, 4)

                ready(pool, f"routes{layer}.1")

                def distances(g, k, first):
                    if not first:
                        pool.wait_ge(s_wps, g + (NG * layer - 3))
                    pool.tensor_tensor(OH2[:, k % 4, :, :], C("iota").unsqueeze(1).to_broadcast([P, 4, NKEYS]),
                                       routesT[:, 1, bass.ds(g * 4, 4)].unsqueeze(2).to_broadcast([P, 4, NKEYS]),
                                       ALU.subtract).then_inc(s_far, 1)

                for g in range(4):
                    distances(g, g, True)
                with pool.Fori(1, NG // 4) as it:
                    for k in range(4):
                        distances(it * 4 + k, k, False)
                if layer == 0:
                    s5_angles()
                    s5_output_map()
                    s5_inputs(0)
                    pooling()
                    s5_inputs(1)

        @block.vector
        def _(dve):
            def step(ins):
                done(dve, ins, v_step)

            def bcast(ap, shape, axis):
                return ap.unsqueeze(axis).to_broadcast(shape)

            def norm_scale(site):
                step(dve.tensor_tensor_reduce(xs[:, 0, :], h[:, 0, :], h[:, 0, :], 1.0, 0.0, ALU.mult, ALU.add,
                                              sm(0, 1)))
                dve.wait_ge(s_square, site + 1)
                step(dve.tensor_scalar(sm(0, 2), sm(0, 2), 1.0 / D, EPS, ALU.mult, ALU.add))
                done(dve, dve.reciprocal(sm(2, 2), sm(0, 2)), s_var)
                dve.wait_ge(s_rstd, site + 1)

            def x_low(site, i):
                B, c0 = i // 2, 4 * (i % 2)
                dve.wait_ge(s_xh, 4 * SPLIT.index(site) + i + 1)
                dve.tensor_tensor(xl[:, c0:c0 + 4, B * P:(B + 1) * P], xnT[:, c0:c0 + 4, B * P:(B + 1) * P],
                                  xh[:, c0:c0 + 4, B * P:(B + 1) * P].bitcast(F32), ALU.subtract).then_inc(s_xl, 1)

            def q_low(layer, m):
                dve.wait_ge(s_qh, HP * layer + m + 1)
                hi, lo = qparts[m % 2]
                dve.tensor_tensor(lo, wq_tile(layer, m), hi.bitcast(F32), ALU.subtract).then_inc(s_ql, 1)

            def gate_low(layer, c):
                dve.wait_ge(s_gh, DC * layer + c + 1)
                hi, lo = gparts[c % 2]
                dve.tensor_tensor(lo, wgate[:, c, :], hi.bitcast(F32), ALU.subtract).then_inc(s_gl, 1)

            def norm(site):
                norm_scale(site)
                done(dve, dve.tensor_scalar(xs[:, 0, :], h[:, 0, :], sm(4, 1), None, ALU.mult), s_xs[0])
                for i in range(4):
                    B, c0 = i // 2, 4 * (i % 2)
                    o = arrive(dve, f"xnT{site}.{i}")
                    w = K(SITES[site], c0, 4)
                    took(dve, dve.tensor_tensor(xnT[:, c0:c0 + 4, B * P:(B + 1) * P],
                                                o[:, :].rearrange("p (c t) -> p c t", c=4),
                                                bcast(w, [P, 4, P], 2), ALU.mult), "dve")
                    if site in SPLIT and i:
                        x_low(site, i - 1)
                if site in SPLIT:
                    x_low(site, 3)

            def add_to_h(name):
                for i in range(4):
                    o = arrive(dve, f"{name}.{i}")
                    hv = h[:, i // 2, 512 * (i % 2):512 * (i % 2) + 512]
                    took(dve, dve.tensor_tensor(hv, hv, o[:, :], ALU.add), "dve")

            def reduce_angle(ang, k):
                step(dve.tensor_scalar(k, ang, 1.0 / TWO_PI, ROUND, ALU.mult, ALU.add))
                step(dve.tensor_scalar(k, k, -ROUND, None, ALU.add))
                for c in (C1, C2, C3):
                    step(dve.scalar_tensor_tensor(out=ang, in0=k, scalar=-c, in1=ang, op0=ALU.mult, op1=ALU.add))
                return dve.tensor_scalar(ang, ang, PI_LOW, -PI_LOW, ALU.min, ALU.max)

            dve.wait_ge(s_x, 16)
            dve.wait_ge(s_const, 48)
            norm(0)
            step(dve.tensor_copy(sm(8, 2), posi[:, :]))
            for B in range(NB):
                step(dve.tensor_scalar(trig[0][:, 32 * B:32 * B + 32], C("freq"), sm(8 + B, 1), None, ALU.mult))
            done(dve, reduce_angle(trig[0], trig[1]), s_rope_ang)
            o = arrive(dve, "zT")
            z3 = gz.rearrange("p (q t) -> p q t", q=2)
            took(dve, dve.tensor_tensor(z3, o[:, :].rearrange("p (q t) -> p q t", q=2),
                                        bcast(K("bup"), [P, 2, SEQ], 2), ALU.add), "dve")
            done(dve, dve.scalar_tensor_tensor(out=ge, in0=gz, scalar=-1.0, in1=gz, op0=ALU.mult, op1=ALU.max), s_log)
            step(dve.tensor_scalar(gz, gz, 0.0, None, ALU.min))
            dve.wait_ge(s_rope_sin, 2)
            step(dve.tensor_tensor(trig[3], trig[3], trig[3], ALU.mult))
            step(dve.tensor_scalar(trig[3], trig[3], -2.0, 1.0, ALU.mult, ALU.add))
            dve.wait_ge(s_loga, 1)
            step(dve.tensor_tensor(gz, gz, gl, ALU.subtract))
            step(dve.tensor_scalar(gz, gz, 1.0 / GATE_NORM, None, ALU.mult))
            for q in range(2):
                step(dve.tensor_tensor_scan(gg[:, 256 * q:256 * q + 256], C("starts"), gz[:, 256 * q:256 * q + 256],
                                            0.0, ALU.mult, ALU.add))
            g3 = gg.rearrange("p (n i) -> p n i", i=CHUNK)
            last3 = g3[:, :, CHUNK - 1]
            step(dve.tensor_scalar(sm(56, 8), last3, 0.5, None, ALU.mult))
            done(dve, dve.tensor_tensor(gd.rearrange("p (n i) -> p n i", i=CHUNK), g3,
                                        bcast(sm(56, 8), [P, 8, CHUNK], 2), ALU.subtract), s_gd)
            step(dve.tensor_copy(sm(64, 8), last3))
            done(dve, dve.tensor_tensor(ge.rearrange("p (n i) -> p n i", i=CHUNK),
                                        bcast(sm(64, 8), [P, 8, CHUNK], 2), g3, ALU.subtract), s_gd)
            done(dve, dve.tensor_copy(sm(72, 2), C("gend")), s_gd)
            dve.wait_ge(s_ge, 5)
            ready(dve, "kaT")
            gate3 = [g.rearrange("p (q t) -> p q t", q=2) for g in (gl, gz, gg, ge)]
            done(dve, dve.tensor_tensor(QT[:, 0:2, :], qraw, gate3[0], ALU.mult), s_qt)
            done(dve, dve.tensor_tensor(KT[:, 0:2, :], kraw, gate3[1], ALU.mult), s_qt)
            done(dve, dve.tensor_tensor(QI[:, 0:2, :], qraw, gate3[2], ALU.mult), s_qt)
            done(dve, dve.tensor_tensor(kraw, kraw, gate3[3], ALU.mult), s_qt)
            dve.wait_ge(s_par_a, 1)
            done(dve, dve.tensor_tensor(sm(116, 16), K("are"), sm(100, 16), ALU.mult), s_par_v)
            done(dve, dve.tensor_tensor(sm(132, 16), K("aim"), sm(100, 16), ALU.mult), s_par_v)
            done(dve, reduce_angle(sm(132, 16), sm(196, 16)), s_par_v)
            dve.wait_ge(s_par_a, 4)
            step(dve.tensor_tensor(sm(180, 16), sm(180, 16), sm(180, 16), ALU.mult))
            step(dve.tensor_scalar(sm(180, 16), sm(180, 16), -2.0, 1.0, ALU.mult, ALU.add))
            step(dve.tensor_tensor(sm(212, 16), sm(148, 16), sm(180, 16), ALU.mult))
            step(dve.tensor_scalar(sm(212, 16), sm(212, 16), -1.0, None, ALU.add))
            step(dve.tensor_tensor(sm(228, 16), sm(148, 16), sm(164, 16), ALU.mult))
            step(dve.tensor_tensor(sm(244, 16), K("are"), K("are"), ALU.mult))
            step(dve.tensor_tensor(sm(260, 16), K("aim"), K("aim"), ALU.mult))
            step(dve.tensor_tensor(sm(244, 16), sm(244, 16), sm(260, 16), ALU.add))
            step(dve.reciprocal(sm(244, 16), sm(244, 16)))
            step(dve.tensor_tensor(sm(276, 16), sm(212, 16), K("are"), ALU.mult))
            step(dve.tensor_tensor(sm(260, 16), sm(228, 16), K("aim"), ALU.mult))
            step(dve.tensor_tensor(sm(276, 16), sm(276, 16), sm(260, 16), ALU.add))
            step(dve.tensor_tensor(sm(276, 16), sm(276, 16), sm(244, 16), ALU.mult))
            step(dve.tensor_tensor(sm(292, 16), sm(228, 16), K("are"), ALU.mult))
            step(dve.tensor_tensor(sm(260, 16), sm(212, 16), K("aim"), ALU.mult))
            step(dve.tensor_tensor(sm(292, 16), sm(292, 16), sm(260, 16), ALU.subtract))
            step(dve.tensor_tensor(sm(292, 16), sm(292, 16), sm(244, 16), ALU.mult))
            step(dve.tensor_scalar(sm(460, 16), sm(276, 16), -1.0, None, ALU.mult))
            done(dve, dve.tensor_scalar(sm(476, 16), sm(292, 16), -1.0, None, ALU.mult), s_coef)
            sinr, cosr = trig[2], trig[3]
            tmp = STATE.rearrange("p n q e -> p (n q e)")
            for B in range(NB):
                ready(dve, f"qkb.{B}")
                xv = QKB[:, B, :].rearrange("p (h two r) -> p h two r", two=2, r=32)
                yv = ROT[:, B, :].rearrange("p (h two r) -> p h two r", two=2, r=32)
                cb_ = bcast(cosr[:, 32 * B:32 * B + 32], [P, 8, 32], 1)
                sb_ = bcast(sinr[:, 32 * B:32 * B + 32], [P, 8, 32], 1)
                t_ = [tmp[:, 256 * i:256 * i + 256].rearrange("p (h r) -> p h r", h=8) for i in range(4)]
                dve.tensor_tensor(t_[0], xv[:, :, 0, :], cb_, ALU.mult).then_inc(v_step, 1)
                dve.tensor_tensor(t_[1], xv[:, :, 1, :], sb_, ALU.mult).then_inc(v_step, 1)
                dve.tensor_tensor(t_[2], xv[:, :, 1, :], cb_, ALU.mult).then_inc(v_step, 1)
                count[v_step] += 3
                step(dve.tensor_tensor(t_[3], xv[:, :, 0, :], sb_, ALU.mult))
                step(dve.tensor_tensor(yv[:, :, 0, :], t_[0], t_[1], ALU.subtract))
                done(dve, dve.tensor_tensor(yv[:, :, 1, :], t_[2], t_[3], ALU.add), s_rot)
            for B in range(NB):
                done(dve, dve.tensor_tensor(KI[:, B, 256:512].rearrange("p (h d) -> p h d", h=4),
                                            ROT[:, B, 256:512].rearrange("p (h d) -> p h d", h=4),
                                            bcast(C("kdec"), [P, 4, HD], 2), ALU.mult), s_ret)
            ready(dve, "rqT")
            qd = C("qdec").rearrange("p (q i) -> p q i", q=2)
            for q in range(2):
                ins = dve.tensor_tensor(QI[:, 2 + q, :].rearrange("p (n i) -> p n i", i=CHUNK),
                                        QT[:, 2 + q, :].rearrange("p (n i) -> p n i", i=CHUNK),
                                        bcast(qd[:, q, :], [P, 4, CHUNK], 1), ALU.mult)
                if q:
                    done(dve, ins, s_ret)
                else:
                    step(ins)
            rm = C("retmask").rearrange("p (h i) -> p h i", h=4)
            for B in range(NB):
                ready(dve, f"sT.{B}")
                v = ST[:, B, 4:8, :]
                done(dve, dve.tensor_tensor(v, v, rm, ALU.mult), s_masked_v)
            for n in range(3):
                o = arrive(dve, f"kv.{n}")
                if n == 0:
                    took(dve, dve.tensor_copy(STATE[:, 0, :, :].rearrange("p q e -> p (q e)"), o[:, :]), "dve")
                else:
                    for q in range(PAIRS):
                        dec = sm(16 + 4 * q + n, 1) if q < 2 else sm(72 + q - 2, 1)
                        ins = dve.scalar_tensor_tensor(out=STATE[:, n, q, :], in0=STATE[:, n - 1, q, :], scalar=dec,
                                                       in1=o[:, P * q:P * q + P], op0=ALU.mult, op1=ALU.add)
                        if q == PAIRS - 1:
                            took(dve, ins, "dve")
                        else:
                            step(ins)
            dve.wait_ge(s_row, 16)
            dve.wait_ge(s_silu, 1)
            step(dve.tensor_tensor(SG, SG, bcast(mix_row, [P, NB, D], 1), ALU.mult))
            for B in range(NB):
                ready(dve, f"o.{2 * B + 1}")
                v = O[:, B, 512:1024].rearrange("p (h e) -> p h e", h=4)
                step(dve.tensor_reduce(sm(80, 4), v, AX_X, ALU.add))
                step(dve.tensor_scalar(sm(80, 4), sm(80, 4), 1.0 / P, None, ALU.mult))
                done(dve, dve.tensor_tensor(v, v, bcast(sm(80, 4), [P, 4, P], 2), ALU.subtract), s_cen)
            for B in range(NB):
                dve.wait_ge(s_sq, B + 1)
                step(dve.tensor_reduce(sm(24 + 8 * B, 8), SQ[:, D * B:D * B + D].rearrange("p (g e) -> p g e", e=P),
                                       AX_X, ALU.add))
            step(dve.tensor_scalar(sm(24, 16), sm(24, 16), 1.0 / P, EPS, ALU.mult, ALU.add))
            done(dve, dve.reciprocal(sm(24, 16), sm(24, 16)), s_hvar)
            dve.wait_ge(s_hrstd, 1)
            for B in range(NB):
                o8 = O[:, B, :].rearrange("p (g e) -> p g e", e=P)
                step(dve.tensor_tensor(o8, o8, bcast(sm(40 + 8 * B, 8), [P, 8, P], 2), ALU.mult))
                done(dve, dve.tensor_tensor(O[:, B, :], O[:, B, :], SG[:, B, :], ALU.mult), s_oready)
            for m in range(2):
                q_low(0, m)
            add_to_h("mix0")

            for layer in range(DEPTH):
                if layer:
                    norm(3)
                    dve.wait_ge(s_sin, 1)
                    step(dve.tensor_tensor(cosE, cosE, cosE, ALU.mult))
                    step(dve.tensor_scalar(cosE, cosE, -2.0, 1.0, ALU.mult, ALU.add))
                    for half in range(2):
                        if half == 0:
                            dve.wait_ge(s_sin, 2)
                            dve.wait_ge(s_c, 1)

                        def scans(j):
                            dve.wait_ge(s_drive, 8 * half + j + 1)
                            mag = sm(148 + 8 * half + j, 1).to_broadcast([P, SEQ])
                            for ri in range(2):
                                step(dve.tensor_tensor_scan(y4[:, ri, j, :], mag, v4[:, ri, j, :], 0.0, ALU.mult, ALU.add))

                        for j in range(8):
                            o = arrive(dve, f"bu.{8 * half + j}")
                            b3 = o[:, :].rearrange("p (r t) -> p r t", r=2)
                            dve.tensor_tensor(y4[:, :, j, :], b3, bcast(cosE[:, 8 * half + j, :], [P, 2, SEQ], 1),
                                              ALU.mult).then_inc(s_turned, 1)
                            took(dve, dve.tensor_tensor(sine_part[j % 2], b3, bcast(sinE[:, 8 * half + j, :], [P, 2, SEQ], 1),
                                                        ALU.mult), "dve")
                            if j:
                                scans(j - 1)
                        scans(7)
                        ready(dve, "ucT.1")
                        for ri in range(2):
                            step(dve.tensor_tensor(v4[:, ri, :, :], y4[:, ri, :, :], cosE[:, 8 * half:8 * half + 8, :], ALU.mult))
                            step(dve.tensor_tensor(w4[:, ri, :, :], y4[:, ri, :, :], sinE[:, 8 * half:8 * half + 8, :], ALU.mult))
                        step(dve.tensor_tensor(v4[:, 0, :, :], v4[:, 0, :, :], w4[:, 1, :, :], ALU.subtract))
                        done(dve, dve.tensor_tensor(v4[:, 1, :, :], v4[:, 1, :, :], w4[:, 0, :, :], ALU.add), s_xst)
                        if half:
                            add_to_h("mixp")
                        o = arrive(dve, f"ys.{half}")
                        for q in range(2):
                            f = 2 * half + q
                            ins = dve.scalar_tensor_tensor(out=Z[:, f, :], in0=UD[:, f, :], scalar=K("dskip", f, 1),
                                                           in1=o[:, 256 * q:256 * q + 256], op0=ALU.mult, op1=ALU.add)
                            if q:
                                took(dve, ins, "dve")
                            else:
                                step(ins)
                    dve.wait_ge(s_z, 1)
                    ready(dve, "glu.1")
                    done(dve, dve.tensor_tensor(MT1[:, 4:8, :], Z, SGL, ALU.mult), s_mt)
                    for m in range(2):
                        q_low(1, m)
                    add_to_h("mix1")

                norm(1 + 3 * layer)
                for m in range(2, HP):
                    q_low(layer, m)
                idx = tk[0].bitcast(U32).rearrange("p (g k) -> p g k", g=HP)
                top = tk[1].rearrange("p (g k) -> p g k", g=HP)
                idf = tk[2].rearrange("p (g k) -> p g k", g=HP)
                for B in range(NB):
                    def top16(vals, index, data, n):
                        for r in range(2):
                            for i in range(n):
                                dve.max(out=vals(i)[:, 8 * r:8 * r + 8], in_=data(i)).then_inc(v_step, 1)
                            count[v_step] += n
                            dve.wait_ge(v_step, count[v_step])
                            for i in range(n):
                                dve.max_index(index(i)[:, 8 * r:8 * r + 8], vals(i)[:, 8 * r:8 * r + 8],
                                              data(i)).then_inc(v_step, 1)
                            count[v_step] += n
                            dve.wait_ge(v_step, count[v_step])
                            if r == 0:
                                for i in range(n):
                                    dve.match_replace(data(i), vals(i)[:, 0:8], data(i), LOWEST).then_inc(v_step, 1)
                                count[v_step] += n
                                dve.wait_ge(v_step, count[v_step])

                    ready(dve, f"scores{layer}.{4 * B + 3}")
                    top16(lambda i: top[:, i, :], lambda i: idx[:, i, :], lambda i: SC[:, B, i, :], HP)
                    step(dve.tensor_copy(tk[2], tk[0].bitcast(U32)))
                    c4 = CAND.rearrange("p h (i j) -> p h i j", i=TOPK)
                    t4 = top.rearrange("p (h two) k -> p h two k", two=2)
                    step(dve.tensor_tensor(c4, bcast(t4[:, :, 0, :], [P, PH, TOPK, TOPK], 3),
                                           bcast(t4[:, :, 1, :], [P, PH, TOPK, TOPK], 2), ALU.add))
                    best = tk[4][:, P * B:P * B + P].rearrange("p (h k) -> p h k", h=PH)
                    flat = tk[3][:, 0:P].bitcast(U32).rearrange("p (h k) -> p h k", h=PH)
                    top16(lambda i: best[:, i, :], lambda i: flat[:, i, :], lambda i: CAND[:, i, :], PH)
                    step(dve.tensor_copy(sm(320, 8), best[:, :, 0]))
                    done(dve, dve.tensor_tensor(best, best, bcast(sm(320, 8), [P, PH, TOPK], 2), ALU.subtract), s_best)
                    fu = tk[3][:, 0:P].bitcast(U32)
                    hi_lo = tk[3][:, P:2 * P].bitcast(U32)
                    id4 = idf.rearrange("p (h two) k -> p h two k", two=2)
                    for side in range(2):
                        if side == 0:
                            step(dve.tensor_scalar(hi_lo, fu, 4, None, ALU.logical_shift_right))
                        else:
                            step(dve.tensor_scalar(hi_lo, fu, TOPK - 1, None, ALU.bitwise_and))
                        which = sm(330, P)
                        step(dve.tensor_copy(which, hi_lo))
                        e4 = EQ.rearrange("p (h k i) -> p h k i", h=PH, k=TOPK)
                        e3 = EQ.rearrange("p (g i) -> p g i", i=TOPK)
                        step(dve.tensor_tensor(e3, bcast(which, [P, P, TOPK], 2), bcast(C("iota16"), [P, P, TOPK], 1),
                                               ALU.is_equal))
                        step(dve.tensor_tensor(e4, e4, bcast(id4[:, :, side, :], [P, PH, TOPK, TOPK], 2), ALU.mult))
                        step(dve.tensor_reduce(tk[5 + side][:, P * B:P * B + P], e3, AX_X, ALU.add))
                dve.wait_ge(s_exp, layer + 1)
                for B in range(NB):
                    best = tk[4][:, P * B:P * B + P].rearrange("p (h k) -> p h k", h=PH)
                    step(dve.tensor_reduce(sm(320, 8), best, AX_X, ALU.add))
                    step(dve.reciprocal(sm(320, 8), sm(320, 8)))
                    done(dve, dve.tensor_tensor(tk[7][:, P * B:P * B + P].rearrange("p (h k) -> p h k", h=PH), best,
                                                bcast(sm(320, 8), [P, PH, TOPK], 2), ALU.mult), s_route)
                ready(dve, f"routes{layer}.1")
                iota = C("iota")

                def onehots(g, k, first):
                    if not first:
                        dve.wait_ge(s_wps, g + (NG * layer - 3))
                    for t in range(4):
                        ins = dve.tensor_scalar(OH1[:, k % 4, t, :], iota, routesT[:, 0, bass.ds(g * 4 + t, 1)],
                                                routesT[:, 2, bass.ds(g * 4 + t, 1)], ALU.is_equal, ALU.mult)
                    ins.then_inc(s_first, 1)

                def times_hidden(g, k):
                    dve.wait_ge(s_wsb, g + (NG * layer + 1))
                    wv = W[:, 0:AHEAD, bass.ds(g * 4, 4)]
                    dve.tensor_tensor(wv, work[k][:, :].rearrange("p (t b) -> p b t", t=4)[:, 0:AHEAD, :], wv,
                                      ALU.mult).then_inc(s_wmul, 1)

                for g in range(4):
                    onehots(g, g, True)
                    if g >= 2:
                        times_hidden(g - 2, g - 2)
                with dve.Fori(1, NG // 4) as it:
                    for k in range(4):
                        onehots(it * 4 + k, k, False)
                        times_hidden(it * 4 + (k - 2), (k - 2) % 4)
                for g in range(NG - 2, NG):
                    times_hidden(g, g % 4)
                b0 = NKEYS * layer
                dve.wait_ge(s_wmul, NG * (layer + 1))

                def low(b, k, hi, lo, from_act, signal):
                    for half in range(2):
                        dve.wait_ge(from_act, b * 2 + (2 * b0 + half + 1))
                        dve.tensor_tensor(lo[half], slot[k][:, 512 * half:512 * half + 512], hi[half].bitcast(F32),
                                          ALU.subtract).then_inc(signal, 1)

                def two_parts(b, s, src):
                    dve.tensor_copy(ph[s], src).then_inc(s_pf, 1)
                    dve.wait_ge(s_pf, b + (b0 + 1))
                    dve.tensor_tensor(pl[s], src, ph[s].bitcast(F32), ALU.subtract).then_inc(s_p, 1)

                def stored(b, q, k):
                    s = k % 2
                    after(dve, s_vused, b * 2 + (2 * b0 - 2))
                    two_parts(b, s, W[:, bass.ds(b, 1), :].rearrange("p o t -> p (o t)"))
                    low(b, k, *halves_of[s], s_vh, s_vl)

                def gate_and_v(b, h_, s):
                    dve.wait_ge(s_gelu, b + (b0 + 1))
                    dve.wait_ge(s_vused, b * 2 + (2 * b0 - 2))
                    dve.tensor_tensor(PF[s], work[s][:, 0:SEQ], W[:, bass.ds(b, 1), :].rearrange("p o t -> p (o t)"),
                                      ALU.mult).then_inc(s_pm, 1)
                    dve.wait_ge(s_pm, b + ((NKEYS - AHEAD) * layer - AHEAD + 1))
                    two_parts(b, s, PF[s])
                    low(b, 2 + s, vh, vl, s_vh, s_vl)

                def u_gate_v(b, h_, s):
                    low(b + 1, 1 - s, uh, ul, s_uh, s_ul)
                    gate_and_v(b, h_, s)

                for b in range(2):
                    stored(b, 0, b)
                over_b(dve, stored, 2, AHEAD - 1, 4)
                low(AHEAD, 0, uh, ul, s_uh, s_ul)
                stored(AHEAD - 1, None, 3)
                over_b(dve, u_gate_v, AHEAD, NKEYS - 1)
                gate_and_v(NKEYS - 1, None, 1)
                gate_low(layer, 0)
                dve.wait_ge(s_vused, 2 * NKEYS * (layer + 1))
                for i in range(4):
                    hv = h[:, i // 2, 512 * (i % 2):512 * (i % 2) + 512]
                    ins = dve.tensor_tensor(hv, hv, sums[i][:, :], ALU.add)
                    if i == 3:
                        done(dve, ins, s_added)
                    else:
                        step(ins)
                norm(2 + 3 * layer)
                for c in range(1, DC):
                    gate_low(layer, c)
                for i in range(4):
                    ready(dve, f"gate{layer}.{i}")
                    gv = GT[:, i // 2, 512 * (i % 2):512 * (i % 2) + 512]
                    hv = h[:, i // 2, 512 * (i % 2):512 * (i % 2) + 512]
                    step(dve.tensor_tensor(gv, gv, EMB[:, i // 2, 512 * (i % 2):512 * (i % 2) + 512], ALU.mult))
                    ins = dve.tensor_tensor(hv, hv, gv, ALU.add)
                    if i == 3:
                        done(dve, ins, s_emb)
                    else:
                        step(ins)
            norm_scale(6)
            dve.wait_ge(s_row, 32)
            for B in range(NB):
                done(dve, dve.scalar_tensor_tensor(out=xs[:, B, :], in0=h[:, B, :], scalar=sm(4 + B, 1),
                                                   in1=final_row, op0=ALU.mult, op1=ALU.mult), s_fin)


def kernel(x, p, positions, norm_mix_w, norm_ffn_w, norm_ple_w, final_norm_w,
           ev_w_in, ev_gla_w_up, ev_gla_b_up, ev_gla_norm_w, ev_ret_norm_w, ev_w_out,
           od_w_in, od_pool_w, od_pool_scale, od_s5_a_re, od_s5_a_im, od_s5_log_dt,
           od_s5_b_re, od_s5_b_im, od_s5_c_re, od_s5_c_im, od_s5_d, od_s5_w_glu, od_s5_b_glu, od_w_out,
           peer_w_q, peer_sub_keys, peer_u, peer_v, ple_w_proj, ple_w_gate):
    import concourse.bacc as bacc
    from concourse.bass_utils import run_bass_kernel_spmd

    def arr(a):
        return np.asarray(a)

    def tiles(a):
        a = arr(a)
        return a.reshape(-1, P, a.shape[-1]).transpose(1, 0, 2)

    def column(a):
        return arr(a).reshape(-1, P).T

    w_in = arr(ev_w_in)[0]
    q_a, k_a, v_a, g_a, r_a, q_b, k_b, v_b, g_b = np.split(
        w_in, np.cumsum([256, 256, 512, 512, GATE_RANK, 256, 256, 512])[:8], axis=1)
    groups = [np.concatenate([q_a, k_a], 1), v_a, g_a, np.concatenate([q_b, k_b], 1), v_b, g_b]
    consts, counts = constants()
    cols = np.concatenate(
        [column(a) for l in range(DEPTH) for a in (arr(norm_mix_w)[l], arr(norm_ffn_w)[l], arr(norm_ple_w)[l])]
        + [column(ev_gla_b_up), column(od_pool_scale), column(od_s5_d), column(od_s5_b_glu), column(od_s5_a_re),
           column(od_s5_a_im), column(np.repeat(arr(od_s5_log_dt).reshape(-1), HD))], axis=1)
    rows = np.concatenate([np.tile(arr(ev_gla_norm_w)[0], 4), arr(ev_ret_norm_w)[0], arr(final_norm_w)])
    s5_b = np.zeros((4, 2, 16, 4, 2, 2, HD), np.float32)
    s5_c = np.zeros((2, HD, 2, S5_TILES, 2, 16), np.float32)
    for r, (b, c) in enumerate(((od_s5_b_re, od_s5_c_re), (od_s5_b_im, od_s5_c_im))):
        b = arr(b)[0].reshape(4, 4, 2, HD, 16)
        c = arr(c)[0].reshape(S5_TILES, 2, 16, HD)
        for g in range(2):
            s5_b[:, g, :, :, r, g, :] = b[:, :, g].transpose(1, 3, 0, 2)
            s5_c[g, :, r, :, g, :] = c[:, g].transpose(2, 0, 1)
    data = {
        "consts": consts, "counts": counts.reshape(P, 4, SEQ), "cols": cols, "rows": np.tile(rows, (P, 1)),
        "pos": arr(positions).reshape(NB, P).T,
        "x": arr(x)[0].reshape(NB, P, D).transpose(1, 0, 2),
        "pT": arr(p)[:, 0].transpose(0, 2, 1).reshape(DEPTH, 2, P, SEQ).transpose(0, 2, 1, 3),
        "w_even": np.stack([tiles(g) for g in groups]), "w_ra": tiles(r_a), "w_up": arr(ev_gla_w_up)[0],
        "w_out0": tiles(arr(ev_w_out)[0]), "w_odd": arr(od_w_in)[0].reshape(DC, P, D),
        "w_pool": arr(od_pool_w)[0].transpose(1, 0, 2),
        "s5_b": s5_b.reshape(P, 4, 2, P), "s5_c": s5_c.reshape(P, 2, S5_TILES, 32),
        "w_glu": tiles(arr(od_s5_w_glu)[0]), "w_out1": tiles(arr(od_w_out)[0]),
        "w_q": np.stack([np.stack([tiles(g) for g in np.split(w, 4, axis=1)]) for w in arr(peer_w_q)]),
        "keys": arr(peer_sub_keys).reshape(DEPTH, HP, NKEYS, P).transpose(0, 3, 1, 2),
        "u_tab": arr(peer_u).reshape(DEPTH, NKEYS, NKEYS, DC, P).transpose(0, 2, 4, 3, 1).reshape(DEPTH, NKEYS, P, D),
        "v_tab": arr(peer_v).reshape(DEPTH, NKEYS, NKEYS, D).transpose(0, 2, 1, 3),
        "w_ple": np.concatenate([arr(ple_w_gate).reshape(DEPTH, DC, P, D), arr(ple_w_proj).reshape(DEPTH, 2, P, D)], 1),
    }
    data = {f"in_{n}": np.ascontiguousarray(a) for n, a in data.items()}
    nc = bacc.Bacc("TRN2", target_bir_lowering=False, num_devices=1)
    args = {n[3:]: nc.dram_tensor(n, a.shape, mybir.dt.from_np(a.dtype), kind="ExternalInput").ap()
            for n, a in data.items()}
    out = nc.dram_tensor("out", (1, SEQ, D), F32, kind="ExternalOutput").ap()
    program(nc, out=out.rearrange("o (b p) d -> p (o b) d", p=P), **args)
    result = run_bass_kernel_spmd(nc, [data], core_ids=[0])
    return result.results[0]["out"]
```
